# Optimizing a Trainium2 kernel written in Bass

```python
import math
import jax, jax.numpy as jnp
from jax import lax
import numpy as np

D_MODEL = 1024
BATCH = 1
SEQ = 1024
DEPTH = 1

N_MEM = 256
EPS = 1e-5
NEG_INF = -1e30
H_A = 8
HD_A = 64
D_A = H_A * HD_A
WIN_DIL = ((128, 1), (512, 4), (2048, 16))
BLK = 128
D_B = D_MODEL - D_A
S5_CH = 16
S5_G = D_B // S5_CH
S5_P = 64
D_IN = 3 * D_A + D_B
NUM_BUCKETS = 32
REL_MAX_DIST = 2048
H_X = 4
HD_X = 128
D_X = H_X * HD_X
N_EXPERTS = 32
TOP_K = 4
D_FF = D_MODEL
SWIGLU_ALPHA = 1.702
SWIGLU_LIMIT = 7.0
MOE_BLOCK = 128

kernel_name = "hybrid_dilated_s5_moe_trunk"

def _rmsnorm(x, g):
    xf = x.astype(jnp.float32)
    y = xf * lax.rsqrt(jnp.mean(xf * xf, axis=-1, keepdims=True) + EPS)
    return (y * g.astype(jnp.float32)).astype(x.dtype)

def _t5_bucket(n):
    max_exact = NUM_BUCKETS // 2
    nf = jnp.maximum(n, 1).astype(jnp.float32)
    large = max_exact + (jnp.log(nf / max_exact) / math.log(REL_MAX_DIST / max_exact)
                         * (NUM_BUCKETS - max_exact)).astype(jnp.int32)
    large = jnp.minimum(large, NUM_BUCKETS - 1)
    return jnp.where(n < max_exact, n, large)

def _dilated_branch(q, k, v, rel_bias, window, dil):
    Bsz, S, H, Dh = q.shape
    steps = window // dil
    span = dil * BLK
    s_pad = -(-S // span) * span
    L = s_pad // dil
    nb = L // BLK

    def to_sub(t):
        t = jnp.pad(t, ((0, 0), (0, s_pad - S), (0, 0), (0, 0)))
        t = t.reshape(Bsz, L, dil, H, Dh).transpose(0, 2, 1, 3, 4)
        return t.reshape(Bsz, dil, nb, BLK, H, Dh)

    def with_prev(t):
        prev = jnp.pad(t[:, :, :-1], ((0, 0), (0, 0), (1, 0), (0, 0), (0, 0), (0, 0)))
        return jnp.concatenate([prev, t], axis=3)

    qs = to_sub(q)
    kb = with_prev(to_sub(k))
    vb = with_prev(to_sub(v))

    qi = jnp.arange(BLK, dtype=jnp.int32)[:, None]
    ki = jnp.arange(2 * BLK, dtype=jnp.int32)[None, :]
    dist = BLK + qi - ki
    in_win = (dist >= 0) & (dist <= steps)
    bias = rel_bias[_t5_bucket(jnp.clip(dist, 0, steps) * dil)]
    bias = bias.transpose(2, 0, 1).astype(jnp.float32)
    has_prev = jnp.arange(nb)[:, None, None] > 0
    mask = in_win[None] & (has_prev | (ki >= BLK)[None])

    s = jnp.einsum('bdnqhe,bdnkhe->bdnhqk', qs, kb,
                   preferred_element_type=jnp.float32) * (Dh ** -0.5) + bias
    s = jnp.where(mask[:, None], s, NEG_INF)
    m = jnp.max(s, axis=-1)
    e = jnp.exp(s - m[..., None])
    den = jnp.sum(e, axis=-1)
    num = jnp.einsum('bdnhqk,bdnkhe->bdnqhe', e, vb.astype(jnp.float32))

    def from_sub(t):
        t = t.reshape((Bsz, dil, L) + t.shape[4:])
        t = jnp.swapaxes(t, 1, 2)
        return t.reshape((Bsz, s_pad) + t.shape[3:])[:, :S]

    return from_sub(num), from_sub(jnp.swapaxes(den, 3, 4)), from_sub(jnp.swapaxes(m, 3, 4))

def _dilated_attention(q, k, v, rel_bias):
    nums, dens, maxs = [], [], []
    for window, dil in WIN_DIL:
        n_, d_, m_ = _dilated_branch(q, k, v, rel_bias, window, dil)
        nums.append(n_)
        dens.append(d_)
        maxs.append(m_)
    ms = jnp.stack(maxs)
    w = jnp.exp(ms - jnp.max(ms, axis=0, keepdims=True))
    num = jnp.einsum('pbsh,pbshe->bshe', w, jnp.stack(nums))
    den = jnp.einsum('pbsh,pbsh->bsh', w, jnp.stack(dens))
    return num / den[..., None]

def _linear_recurrence(left, right):
    a_l, b_l = left
    a_r, b_r = right
    return a_r * a_l, a_r * b_l + b_r

def _s5_mixer(u, a_re, a_im, b_re, b_im, c_re, c_im, log_dt, d_skip, w_glu, b_glu):
    f32 = jnp.float32
    Bsz, S, _ = u.shape
    uf = u.astype(f32).reshape(Bsz, S, S5_G, S5_CH)
    lam = lax.complex(a_re.astype(f32), a_im.astype(f32))
    dt = jnp.exp(log_dt.astype(f32))[:, None]
    a_bar = jnp.exp(lam * dt)
    b_bar = ((a_bar - 1.0) / lam)[..., None] * lax.complex(b_re.astype(f32), b_im.astype(f32))
    bu = jnp.einsum('gpc,bsgc->bsgp', b_bar, uf.astype(jnp.complex64))
    a = jnp.broadcast_to(a_bar, bu.shape)
    _, state = lax.associative_scan(_linear_recurrence, (a, bu), axis=1)
    c = lax.complex(c_re.astype(f32), c_im.astype(f32))
    y = jnp.einsum('gcp,bsgp->bsgc', c, state).real + d_skip.astype(f32).reshape(S5_G, S5_CH) * uf
    y = jax.nn.gelu(y.reshape(Bsz, S, D_B), approximate=False)
    gate = jax.nn.sigmoid(y @ w_glu.astype(f32) + b_glu.astype(f32))
    return (y * gate).astype(u.dtype)

def _memory_attention(hn, mem_n, w_q, w_kv, w_o):
    Bsz, S, _ = hn.shape
    n_mem = mem_n.shape[1]
    q = (hn @ w_q).reshape(Bsz, S, H_X, HD_X)
    kv = (mem_n @ w_kv).reshape(Bsz, n_mem, 2, H_X, HD_X)
    k, v = kv[:, :, 0], kv[:, :, 1]
    s = jnp.einsum('bshe,bmhe->bhsm', q, k, preferred_element_type=jnp.float32) * (HD_X ** -0.5)
    p = jax.nn.softmax(s, axis=-1)
    o = jnp.einsum('bhsm,bmhe->bshe', p.astype(v.dtype), v).reshape(Bsz, S, D_X)
    return o @ w_o

def _moe(hn, w_router, b_router, w1, b1, w2, b2):
    Bsz, S, D = hn.shape
    T = Bsz * S
    TK = T * TOP_K
    xt = hn.reshape(T, D)
    logits = jnp.einsum('td,de->te', xt, w_router,
                        preferred_element_type=jnp.float32) + b_router.astype(jnp.float32)
    top_val, top_idx = lax.top_k(logits, TOP_K)
    gates = jax.nn.softmax(top_val, axis=-1)
    flat_e = top_idx.reshape(TK)
    order = jnp.argsort(flat_e)
    e_sorted = flat_e[order]
    tok_sorted = order // TOP_K
    g_sorted = gates.reshape(TK)[order]
    counts = jnp.bincount(flat_e, length=N_EXPERTS)
    padded = (counts + MOE_BLOCK - 1) // MOE_BLOCK * MOE_BLOCK
    start = jnp.cumsum(counts) - counts
    pend = jnp.cumsum(padded)
    pstart = pend - padded
    dest = pstart[e_sorted] + jnp.arange(TK, dtype=jnp.int32) - start[e_sorted]
    n_rows = TK + N_EXPERTS * MOE_BLOCK
    n_blk = n_rows // MOE_BLOCK
    xpad = jnp.zeros((n_rows, D), hn.dtype).at[dest].set(xt[tok_sorted])
    blk_e = jnp.minimum(jnp.searchsorted(pend, jnp.arange(n_blk) * MOE_BLOCK, side='right'),
                        N_EXPERTS - 1)

    def expert_block(args):
        xb, e = args
        hb = xb @ w1[e] + b1[e]
        x_glu = jnp.minimum(hb[:, :D_FF], SWIGLU_LIMIT)
        x_lin = jnp.clip(hb[:, D_FF:], -SWIGLU_LIMIT, SWIGLU_LIMIT)
        act = x_glu * jax.nn.sigmoid(SWIGLU_ALPHA * x_glu) * (x_lin + 1.0)
        return act @ w2[e] + b2[e]

    out = lax.map(expert_block, (xpad.reshape(n_blk, MOE_BLOCK, D), blk_e)).reshape(n_rows, D)
    y = jax.ops.segment_sum(out[dest] * g_sorted[:, None].astype(out.dtype), tok_sorted,
                            num_segments=T)
    return y.reshape(Bsz, S, D)

def setup_inputs(seed: int = 0) -> dict:
    key = jax.random.key(seed)
    ks = iter(jax.random.split(key, 40))

    def nrm(shape, scale):
        return scale * jax.random.normal(next(ks), shape, jnp.float32)

    def gain(shape):
        return 1.0 + nrm(shape, 0.01)

    L = DEPTH
    n_idx = jnp.arange(S5_P, dtype=jnp.float32)
    return {
        "x": nrm((BATCH, SEQ, D_MODEL), 1.0),
        "mem": nrm((BATCH, N_MEM, D_MODEL), 1.0),
        "rel_bias": nrm((NUM_BUCKETS, H_A), 0.2),
        "norm_mix": gain((L, D_MODEL)),
        "w_in": nrm((L, D_MODEL, D_IN), D_MODEL ** -0.5),
        "s5_a_re": -0.5 + nrm((L, S5_G, S5_P), 0.01),
        "s5_a_im": math.pi * n_idx + nrm((L, S5_G, S5_P), 0.01),
        "s5_b_re": nrm((L, S5_G, S5_P, S5_CH), (2 * S5_CH) ** -0.5),
        "s5_b_im": nrm((L, S5_G, S5_P, S5_CH), (2 * S5_CH) ** -0.5),
        "s5_c_re": nrm((L, S5_G, S5_CH, S5_P), (2 * S5_P) ** -0.5),
        "s5_c_im": nrm((L, S5_G, S5_CH, S5_P), (2 * S5_P) ** -0.5),
        "s5_log_dt": jax.random.uniform(next(ks), (L, S5_G), jnp.float32,
                                        math.log(1e-3), math.log(1e-1)),
        "s5_d": nrm((L, D_B), 1.0),
        "w_glu": nrm((L, D_B, D_B), D_B ** -0.5),
        "b_glu": nrm((L, D_B), 0.01),
        "g_out_attn": gain((L, D_A)),
        "g_out_ssm": gain((L, D_B)),
        "w_out": nrm((L, D_MODEL, D_MODEL), D_MODEL ** -0.5),
        "norm_xattn": gain((L, D_MODEL)),
        "norm_mem": gain((L, D_MODEL)),
        "w_xq": nrm((L, D_MODEL, D_X), D_MODEL ** -0.5),
        "w_xkv": nrm((L, D_MODEL, 2 * D_X), D_MODEL ** -0.5),
        "w_xo": nrm((L, D_X, D_MODEL), D_X ** -0.5),
        "norm_moe": gain((L, D_MODEL)),
        "w_router": nrm((L, D_MODEL, N_EXPERTS), D_MODEL ** -0.5),
        "b_router": nrm((L, N_EXPERTS), 0.01),
        "w1": nrm((L, N_EXPERTS, D_MODEL, 2 * D_FF), D_MODEL ** -0.5),
        "b1": nrm((L, N_EXPERTS, 2 * D_FF), 0.01),
        "w2": nrm((L, N_EXPERTS, D_FF, D_MODEL), D_FF ** -0.5),
        "b2": nrm((L, N_EXPERTS, D_MODEL), 0.01),
        "norm_final": gain((D_MODEL,)),
    }

def reference(x, mem, rel_bias, norm_mix, w_in, s5_a_re, s5_a_im, s5_b_re, s5_b_im, s5_c_re, s5_c_im,
              s5_log_dt, s5_d, w_glu, b_glu, g_out_attn, g_out_ssm, w_out, norm_xattn, norm_mem,
              w_xq, w_xkv, w_xo, norm_moe, w_router, b_router, w1, b1, w2, b2, norm_final):
    Bsz, S, _ = x.shape
    h = x
    for l in range(DEPTH):
        xn = _rmsnorm(h, norm_mix[l])
        proj = xn @ w_in[l]
        q = proj[..., 0:D_A].reshape(Bsz, S, H_A, HD_A)
        k = proj[..., D_A:2 * D_A].reshape(Bsz, S, H_A, HD_A)
        v = proj[..., 2 * D_A:3 * D_A].reshape(Bsz, S, H_A, HD_A)
        u = proj[..., 3 * D_A:]
        y_a = _dilated_attention(q, k, v, rel_bias).reshape(Bsz, S, D_A).astype(h.dtype)
        y_b = _s5_mixer(u, s5_a_re[l], s5_a_im[l], s5_b_re[l], s5_b_im[l], s5_c_re[l], s5_c_im[l],
                        s5_log_dt[l], s5_d[l], w_glu[l], b_glu[l])
        mix = jnp.concatenate([_rmsnorm(y_a, g_out_attn[l]), _rmsnorm(y_b, g_out_ssm[l])], axis=-1)
        h = h + mix @ w_out[l]
        h = h + _memory_attention(_rmsnorm(h, norm_xattn[l]), _rmsnorm(mem, norm_mem[l]),
                                  w_xq[l], w_xkv[l], w_xo[l])
        h = h + _moe(_rmsnorm(h, norm_moe[l]), w_router[l], b_router[l], w1[l], b1[l], w2[l], b2[l])
    return _rmsnorm(h, norm_final)


_drawn_inputs = setup_inputs


def setup_inputs(seed=0):
    import zlib

    import numpy as np

    out = dict(_drawn_inputs(seed))
    spreads = {}
    factors = {'s5_a_re': 64.0,
     'b_glu': 5.786,
     'g_out_attn': 3.736,
     'g_out_ssm': 3.739,
     'norm_xattn': 8.0,
     'norm_mem': 8.0,
     'b1': 64.0,
     'b2': 64.0,
     'norm_final': 30.762,
     'norm_moe': 8.0,
     'b_router': 8.0}
    for name, (base, spread) in spreads.items():
        noise = np.random.default_rng([zlib.crc32(name.encode()), seed]).standard_normal(out[name].shape)
        drawn = base * np.exp(spread * noise) if base else spread * noise
        out[name] = __import__('jax').numpy.asarray(drawn.astype(out[name].dtype))
    for name, factor in factors.items():
        out[name] = (out[name] * factor).astype(out[name].dtype)
    return out
```

```python
import math
from collections import namedtuple
from contextlib import ExitStack

import numpy as np

import concourse.bass as bass
from concourse import mybir

F32 = mybir.dt.float32
I32 = mybir.dt.int32
U32 = mybir.dt.uint32
ACT = mybir.ActivationFunctionType
ALU = mybir.AluOpType
AX = mybir.AxisListType

P = 128
D = 1024
S = 1024
NB = S // P
KC = D // P
EPS = 1e-5
NEG = -1e30
H_A, HD_A = 8, 64
D_A = H_A * HD_A
WIN_DIL = ((128, 1), (512, 4), (2048, 16))
NUM_BUCKETS, REL_MAX = 32, 2048
D_B = D - D_A
MB = D_B // P
CH = 16
G = D_B // CH
ST = 64
T = 8
J = S // T
N_MEM, H_X, HD_X = 256, 4, 128
E, TOPK, F = 32, 4, 1024
LIMIT, ALPHA = 7.0, 1.702
LINE = 1152
WIN = 256
NWIN = S // WIN
WIDTHS = (64, 128, 192, 256)
DUMP = S
KB = 1024
BASE = 16640

ONEHOT_ROWS = NUM_BUCKETS + 1


def shape_constants():
    dist = S - 1 - np.arange(LINE)
    n = np.maximum(dist, 0)
    exact = NUM_BUCKETS // 2
    nf = np.maximum(n, 1).astype(np.float32)
    scale = np.float32(math.log(REL_MAX / exact))
    large = exact + (np.log(nf / np.float32(exact)) / scale * np.float32(NUM_BUCKETS - exact)).astype(np.int32)
    bucket = np.where(n < exact, n, np.minimum(large, NUM_BUCKETS - 1))
    held = sum(((dist % d == 0) & (dist >= 0) & (dist <= w)).astype(np.float64) for w, d in WIN_DIL)
    table = np.zeros((ONEHOT_ROWS, LINE), np.float32)
    table[bucket, np.arange(LINE)] = 1.0
    table[NUM_BUCKETS] = np.where(held > 0, np.log(np.maximum(held, 1)), NEG)
    return table


class Chain:

    def __init__(self, eng, sem):
        self.eng, self.sem, self.n = eng, sem, 0

    def step(self, ins):
        self.n += 1
        ins.then_inc(self.sem, 1)
        return self.n

    def link(self, ins):
        self.eng.wait_ge(self.sem, self.step(ins))


def memory(nc, ctx):
    m = {}

    def at(name, kib, shape, dt=F32):
        t = nc.alloc_sbuf_tensor_at(name, shape, dt, offset=BASE + int(kib * KB))
        m[name] = t
        return t

    at("qT", 0, [P, D_A // P, S])
    at("kT", 16, [P, D_A // P, S])
    at("v", 32, [P, NB, D_A])
    at("uT", 0, [P, MB, S])
    at("kmT", 48, [P, H_X, N_MEM])
    at("vm", 52, [P, N_MEM // P, H_X * HD_X])
    off = [56 * KB]

    def small(name, shape, dt=F32):
        t = nc.alloc_sbuf_tensor_at(name, shape, dt, offset=BASE + off[0])
        off[0] += -(-(int(np.prod(shape[1:])) * 4) // 32) * 32
        assert off[0] <= 64 * KB, name
        m[name] = t

    small("ident", [P, P])
    small("b1T", [P, E * 16])
    small("b2T", [P, E * KC])
    small("g_mix", [P, KC])
    small("g_x", [P, KC])
    small("g_mem", [P, KC])
    small("g_moe", [P, KC])
    small("g_oa", [P, D_A // P])
    small("g_ob", [P, MB])
    small("bglu", [P, MB])
    small("dskip", [P, G])
    small("ss", [P, 32])
    small("rs", [P, 32])
    small("ones", [P, P])
    small("neg", [P, 4])
    small("half", [P, 1])
    small("negx", [P, 8])
    small("denx", [P, 8])
    small("den", [P, 4])
    small("a8", [P, 3, G])
    small("cnt_i", [1, E], I32)
    at("xrow", 64, [P, NB, D])
    at("memrow", 80, [P, N_MEM // P, D])
    at("xnT", 96, [P, KC, S])
    for i in range(2):
        at(f"wa{i}", 128 + 16 * i, [P, KC, 512])
    at("memT", 160, [P, KC, N_MEM])
    at("junk", 160, [P, D])
    at("bn", 164, [P, 6, P])
    at("Cp", 169, [P, G, (T + 1) * CH])
    at("CrCi", 187, [P, 2, G * CH])
    at("Bri", 191, [P, 2, G, CH])
    at("lam", 195, [G, 16, ST])
    at("bb", 195, [P, 2, G, CH])
    at("tmp", 199, [P, 2, G * CH])
    at("Cn", 203, [P, 4, 2, P])
    at("BT", 64, [P, G, P])
    at("Pw", 88, [P, T + 1, 2, G])
    at("F12", 90.5, [P, 2, T + 1, G])
    at("G12", 93, [P, 2, T, G])
    at("prm", 95.25, [P, 4, G])
    at("Bm", 80, [P, G, 192])
    at("M1", 104, [P, G, P])
    at("Krow", 120, [CH, G, P])
    at("V", 120, [P, J + 1, 2, G])
    at("U", 187, [P, G, J])
    at("Y1", 64, [P, G, J])
    at("ztile", 136, [CH, G, 112])
    at("bias", 80, [P, H_A, S])
    at("sc", 152.5, [P, 2, S])
    at("pr", 112, [P, 2, S])
    at("prT", 160.5, [P, 2, 512])
    at("ya", 187, [P, NB, D_A])
    at("scan_t", 203, [P, 2, 2, G])
    at("ohb", 152.5, [ONEHOT_ROWS, LINE])
    at("rb", 157.5, [ONEHOT_ROWS, H_A])
    at("line", 158, [H_A, LINE])
    for i in range(3):
        at(f"wd{i}", 16 * i, [P, KC, 512])
    at("h", 80, [P, NB, D])
    at("yaT", 120, [P, D_A // P, S])
    at("yg", 152.5, [P, G, J])
    at("yT", 136, [P, MB, T, J])
    at("ybT", 152.5, [P, MB, S])
    at("gate_s", 187, [P, MB, S])
    at("sq", 169, [P, MB, S])
    at("hT", 120, [P, KC, S])
    at("xn", 64, [P, 4, D])
    at("qxT", 152.5, [P, H_X, S])
    at("xnb", 187, [P, 4, D])
    at("px", 169, [P, 8, N_MEM])
    at("pxT", 177, [P, 2, 512])
    at("oT", 187, [P, H_X, S])
    at("junkd", 203, [P, D])
    at("wr", 112, [P, KC, E])
    at("br", 113.5, [1, E])
    at("logit", 152.5, [P, NB, E])
    at("top8", 154, [P, NB, 8])
    at("idx8", 154.5, [P, NB, 8], U32)
    at("idxf", 155, [P, NB, 8])
    at("gates", 155.5, [P, NB, 8])
    at("gsum", 156, [P, 2, NB])
    at("m4", 156.25, [P, NB, TOPK, E])
    at("maskE", 160.5, [P, NB, E])
    at("rank", 161.5, [P, NB, E])
    at("pref", 162.5, [P, NB + 1, E])
    at("tri", 164, [P, P])
    at("iota_e", 164.5, [P, E])
    at("iota_w", 165, [P, WIN])
    at("dest", 166, [P, 4, NB * TOPK])
    at("desti", 166.75, [P, 2, NB * TOPK], I32)
    at("tok1", 167.25, [P, NB])
    at("dumpid", 167.5, [P, WIN])
    at("lo", 187, [P, 4, P])
    at("hi", 189, [P, 4, 2, WIN])
    m["we"] = [at(f"we{i}", 8 * i if i < 6 else 80 + 8 * (i - 6), [P, KC, WIN]) for i in range(12)]
    at("xg0", 64, [P, D])
    at("xg1", 68, [P, D])
    at("xT", 72, [P, KC, WIN])
    at("act", 128, [P, KC, WIN])
    at("outT", 136, [P, KC, WIN])
    at("orow0", 144, [P, D])
    at("orow1", 148, [P, D])
    at("list_f", 169, [P, 2, WIN])
    at("idx_g", 171, [P, WIN], I32)
    at("idx_s", 172, [P, WIN], I32)
    at("gate_l", 173, [P, WIN])
    at("list_t", 174, [P, 2, WIN])
    at("xlin", 176, [P, 2, 2, WIN])
    at("sg", 180, [P, 2, WIN])
    at("gx", 182, [P, 2], I32)
    at("sx", 182.25, [P, 2], I32)
    at("fin", 0, [P, NB, D])
    at("fout", 80, [P, NB, D])
    at("gfin", 112, [P, D])
    at("jf", 116, [P, D])
    m["ps"] = ctx.enter_context(nc.psum_tensor("ps", [P, 8, 512], F32))
    return namedtuple("Memory", m)(**m)


def chunked(w, cols):
    return w[:, cols].rearrange("(k p) n -> p k n", p=P)


def root(nc, m, ch, col, width, n=1):
    cols = slice(col, col + n)
    ch.link(nc.gpsimd.tensor_scalar(m.ss[:, cols], m.ss[:, cols], width * EPS, None, ALU.add))
    ch.link(nc.gpsimd.tensor_tensor(m.rs[:, cols], m.ss[:, cols], m.half[:, 0:1].to_broadcast([P, n]), ALU.pow))
    return nc.gpsimd.tensor_scalar(m.rs[:, cols], m.rs[:, cols], math.sqrt(width), None, ALU.mult)


def phase_a(nc, block, m, a, sem):
    x_in = [sem(f"x_in{b}") for b in range(NB)]
    mem_in, par_in, c_in, b_in, gain_in, bn_in = (sem(n) for n in ("mem_in", "par_in", "c_in", "b_in", "gain_in", "bn_in"))
    w_in = [sem(f"wa_in{i}") for i in range(6)]
    ident_ok, squared, rooted, scaled, transposed = (sem(n) for n in ("ident_ok", "squared", "rooted", "scaled", "transposed"))
    tr_act, tr_dve, pj_act, pj_dve, grouped = (sem(n) for n in ("tr_act", "tr_dve", "pj_act", "pj_dve", "grouped"))
    u_out, lam_ok, lam_act, s5_step, act_step, prep_ok = (sem(n) for n in ("u_out", "lam_ok", "lam_act", "s5_step", "act_step", "prep_ok"))
    lam_inv = sem("lam_inv")
    units = [(a.w_in, slice(3 * D_A, 4 * D_A)), (a.w_in, slice(D_A, 2 * D_A)), (a.w_in, slice(2 * D_A, 3 * D_A)),
             (a.w_in, slice(0, D_A)), (a.w_xkv, slice(0, 512)), (a.w_xkv, slice(512, 1024))]
    PRM, CRE, B1G, B2G, MEMG = 16, 17, 19, 20, 21

    @block.sync
    def _(sp):
        sp.dma_start(m.xrow[:, 0], a.x[0:P]).then_inc(x_in[0], 16)
        for b in range(1, NB):
            sp.dma_start(m.xrow[:, b], a.x[b * P:(b + 1) * P]).then_inc(x_in[b], 16)
            if b in (3, 7):
                n = b // 4
                sp.dma_start(m.wa0[:] if n == 0 else m.wa1[:], chunked(*units[n])).then_inc(w_in[n], 16)
        sp.wait_ge(transposed, 16)
        sp.dma_start(m.memrow[:], a.mem.rearrange("(b p) d -> p b d", p=P)).then_inc(mem_in, 16)
        for n in range(2, 6):
            sp.wait_ge(grouped, 8 * (n - 1))
            sp.dma_start((m.wa0 if n % 2 == 0 else m.wa1)[:], chunked(*units[n])).then_inc(w_in[n], 16)
            if n == 2:
                sp.wait_ge(pj_act, 4)
                sp.wait_ge(pj_dve, 4)
                sp.dma_start(a.u_dram.rearrange("(m p) n -> p m n", p=P), m.uT[:]).then_inc(u_out, 16)
        sp.wait_ge(u_out, 16)

    def tr_evac(j, out_scale):
        bank = m.ps[:, j % 4, :]
        if j < 16:
            half, k = divmod(j, 8)
            return m.xnT[:, k, half * 512:(half + 1) * 512], bank, m.g_mix[:, k:k + 1]
        if j == PRM:
            return m.prm[:, :, :], m.ps[:, j % 4, 0:P].rearrange("p (q g) -> p q g", g=G), None
        if j in (CRE, CRE + 1):
            return m.CrCi[:, j - CRE, :], bank, None
        if j == B1G:
            return m.b1T[:, :], bank, None
        if j == B2G:
            return m.b2T[:, :], m.ps[:, j % 4, 0:256], None
        k = j - MEMG
        return m.memT[:, k, :], m.ps[:, j % 4, 0:N_MEM], m.g_mem[:, k:k + 1]

    def proj_dst(i):
        bank = m.ps[:, 4 + i % 4, :]
        if i < 8:
            c, half = divmod(i, 2)
            dst = m.uT[:, c, :].rearrange("p (s j) -> p j s", s=T)[:, half * (J // 2):(half + 1) * (J // 2), :]
            return dst, bank.rearrange("p (j s) -> p j s", s=T), 1.0
        if i < 16:
            c, half = divmod(i - 8, 2)
            return m.kT[:, c, half * 512:(half + 1) * 512], bank, 1.0
        if i < 24:
            return m.v[:, i - 16, :], bank, 1.0
        if i < 32:
            c, half = divmod(i - 24, 2)
            return m.qT[:, c, half * 512:(half + 1) * 512], bank, HD_A ** -0.5
        if i < 36:
            return m.kmT[:, i - 32, :], m.ps[:, 4 + i % 4, 0:N_MEM], 1.0
        return m.vm[:, i - 36, :], bank, 1.0

    @block.scalar
    def _(act):
        for dst, src in ((m.g_mix, a.norm_mix), (m.g_x, a.norm_xattn), (m.g_mem, a.norm_mem), (m.g_moe, a.norm_moe),
                         (m.g_oa, a.g_out_attn), (m.g_ob, a.g_out_ssm), (m.bglu, a.b_glu)):
            act.dma_start(dst[:], src.rearrange("(k p) -> p k", p=P)).then_inc(gain_in, 16)
        act.dma_start(m.lam[:, 0, :], a.s5_a_re).then_inc(par_in, 16)
        act.dma_start(m.lam[:, 1, :], a.s5_a_im).then_inc(par_in, 16)
        act.dma_start(m.lam[:, 2, 0:1], a.s5_log_dt.rearrange("(g a) -> g a", a=1)).then_inc(par_in, 16)
        for r, src in enumerate((a.s5_c_re, a.s5_c_im)):
            for dup in range(2):
                act.dma_start(m.Cn[:, :, r, dup * ST:(dup + 1) * ST],
                              src.rearrange("g c p -> (g c) p").rearrange("(i q) p -> q i p", i=4)).then_inc(c_in, 16)
        for r, src in enumerate((a.s5_b_re, a.s5_b_im)):
            for dup in range(2):
                act.dma_start(m.Bri[dup * ST:(dup + 1) * ST, r], src.rearrange("g p c -> p g c")).then_inc(b_in, 16)
        act.dma_start(m.bn[:, 0:4], a.b1.rearrange("e (c f) -> (e c) f", f=P).rearrange("(i q) f -> q i f", i=4)).then_inc(bn_in, 16)
        act.dma_start(m.bn[:, 4:6], a.b2.rearrange("e (c f) -> (e c) f", f=P).rearrange("(i q) f -> q i f", i=2)).then_inc(bn_in, 16)
        for t in range(T):
            act.dma_start(m.dskip[t * CH:(t + 1) * CH, :], a.s5_d.rearrange("(g c) -> c g", c=CH)).then_inc(gain_in, 16)
        for b in range(NB):
            act.wait_ge(x_in[b], 16)
            if b:
                act.wait_ge(squared, b)
            nc.scalar.activation(m.junk[:], m.xrow[:, b], ACT.Square, accum_out=m.ss[:, b:b + 1]).then_inc(squared, 1)

        def evac_tr(j):
            act.wait_ge(transposed, j + 1)
            dst, src, g = tr_evac(j, None)
            nc.scalar.activation(dst, src, ACT.Copy if g is None else ACT.Identity, **({} if g is None else {"scale": g})).then_inc(tr_act, 1)

        def evac_pj(i):
            act.wait_ge(grouped, i + 1)
            if i == 24:
                act.wait_ge(u_out, 16)
            dst, src, s = proj_dst(i)
            nc.scalar.activation(dst, src, ACT.Copy, scale=s).then_inc(pj_act, 1)

        act.wait_ge(gain_in, 16 * 15)
        for j in range(0, 16, 2):
            evac_tr(j)
            if j == 2:
                act.wait_ge(par_in, 48)
                nc.scalar.activation(m.lam[:, 2, 1:2], m.lam[:, 2, 0:1], ACT.Exp).then_inc(lam_act, 1)
            if j == 8:
                act.wait_ge(lam_ok, 1)
                nc.scalar.activation(m.lam[:, 5, :], m.lam[:, 3, :], ACT.Exp).then_inc(lam_act, 1)
        act.wait_ge(lam_ok, 2)
        nc.scalar.activation(m.lam[:, 8, :], m.lam[:, 6, :], ACT.Sin).then_inc(lam_act, 1)
        nc.scalar.activation(m.lam[:, 9, :], m.lam[:, 7, :], ACT.Sin).then_inc(lam_act, 1)
        for j in (16, 18, 20):
            evac_tr(j)
        for i in range(0, 32, 2):
            evac_pj(i)
        for b in range(N_MEM // P):
            act.wait_ge(mem_in, 16)
            act.wait_ge(squared, NB + b)
            nc.scalar.activation(m.junk[:], m.memrow[:, b], ACT.Square, accum_out=m.ss[:, NB + b:NB + b + 1]).then_inc(squared, 1)
        for j in range(22, 29, 2):
            evac_tr(j)
        for i in range(32, 38, 2):
            evac_pj(i)

    @block.vector
    def _(dve):
        def norm(b, row):
            dve.wait_ge(rooted, b + 1)
            nc.vector.tensor_scalar(row, row, m.rs[:, b:b + 1], None, ALU.mult).then_inc(scaled, 1)

        def evac_tr(j):
            dve.wait_ge(transposed, j + 1)
            dst, src, g = tr_evac(j, None)
            if g is None:
                nc.vector.tensor_copy(dst, src).then_inc(tr_dve, 1)
            else:
                nc.vector.tensor_scalar(dst, src, g, None, ALU.mult).then_inc(tr_dve, 1)

        def evac_pj(i):
            dve.wait_ge(grouped, i + 1)
            if i == 25:
                dve.wait_ge(u_out, 16)
            dst, src, s = proj_dst(i)
            nc.vector.tensor_scalar(dst, src, s, None, ALU.mult).then_inc(pj_dve, 1)

        for b in range(4):
            norm(b, m.xrow[:, b])
        dve.wait_ge(gain_in, 16 * 15)
        for j in (1, 3, 5, 7):
            evac_tr(j)
            norm(4 + j // 2, m.xrow[:, 4 + j // 2])
        for j in range(9, 16, 2):
            evac_tr(j)
        dve.wait_ge(lam_ok, 3)
        nc.vector.reciprocal(m.lam[:, 6, :], m.lam[:, 6, :]).then_inc(lam_inv, 1)
        for j in (17, 19):
            evac_tr(j)
        for i in range(1, 32, 2):
            evac_pj(i)
        for b in range(N_MEM // P):
            norm(NB + b, m.memrow[:, b])
        for j in range(21, 29, 2):
            evac_tr(j)
        for i in range(33, 38, 2):
            evac_pj(i)

    @block.tensor
    def _(pe):
        pe.wait_ge(ident_ok, 2)

        def free_bank(j):
            if j >= 4:
                pe.wait_ge(tr_act if j % 2 == 0 else tr_dve, (j - 4) // 2 + 1)

        def put(j, sources, width=P):
            free_bank(j)
            for i, src in enumerate(sources):
                rows = src.shape[0]
                last = nc.tensor.transpose(m.ps[:, j % 4, i * width:i * width + rows], src, m.ident[0:rows, 0:rows])
            last.then_inc(transposed, 1)

        for half in range(2):
            pe.wait_ge(scaled, 4 * (half + 1))
            for k in range(KC):
                put(8 * half + k, [m.xrow[:, 4 * half + i, k * P:(k + 1) * P] for i in range(4)])
        pe.wait_ge(prep_ok, 1)
        put(PRM, [m.lam[:, 8 + 2 * q:10 + 2 * q, :].rearrange("g a p -> g (a p)") for q in range(4)], width=G)
        pe.wait_ge(c_in, 64)
        for r in range(2):
            put(CRE + r, [m.Cn[:, i, r, :] for i in range(4)])
        pe.wait_ge(bn_in, 32)
        put(B1G, [m.bn[:, i] for i in range(4)])
        put(B2G, [m.bn[:, 4 + i] for i in range(2)])

        group = [0]

        def project(weights, moving, width):
            i = group[0]
            if i >= 4:
                pe.wait_ge(pj_act if i % 2 == 0 else pj_dve, (i - 4) // 2 + 1)
            for k in range(KC):
                last = nc.tensor.matmul(m.ps[:, 4 + i % 4, 0:width], weights(k), moving(k), start=(k == 0), stop=(k == KC - 1))
            group[0] += 1
            return last.then_inc(grouped, 1)

        pe.wait_ge(tr_act, 8)
        pe.wait_ge(tr_dve, 8)
        for n in range(4):
            w = m.wa0 if n % 2 == 0 else m.wa1
            pe.wait_ge(w_in[n], 16)
            if n == 2:
                for b in range(NB):
                    project(lambda k: m.xnT[:, k, b * P:(b + 1) * P], lambda k: w[:, k, :], 512)
            else:
                for c in range(4):
                    for half in range(2):
                        project(lambda k: w[:, k, c * P:(c + 1) * P],
                                       lambda k: m.xnT[:, k, half * 512:(half + 1) * 512], 512)
        pe.wait_ge(scaled, NB + 2)
        for k in range(KC):
            put(MEMG + k, [m.memrow[:, b, k * P:(k + 1) * P] for b in range(2)])
        pe.wait_ge(tr_act, 15)
        pe.wait_ge(tr_dve, 14)
        pe.wait_ge(w_in[4], 16)
        for c in range(H_X):
            project(lambda k: m.wa0[:, k, c * P:(c + 1) * P], lambda k: m.memT[:, k, :], N_MEM)
        pe.wait_ge(w_in[5], 16)
        for b in range(2):
            project(lambda k: m.memT[:, k, b * P:(b + 1) * P], lambda k: m.wa1[:, k, :], 512)

    @block.gpsimd
    def _(pool):
        nc.gpsimd.memset(m.ident[:], 0.0).then_inc(ident_ok, 1)
        pool.wait_ge(ident_ok, 1)
        nc.gpsimd.affine_select(out=m.ident[:], in_=m.ident[:], compare_op=ALU.not_equal, fill=1.0, base=0,
                                pattern=[[-1, P]], channel_multiplier=1).then_inc(ident_ok, 1)
        nc.gpsimd.memset(m.ones[:], 1.0)
        ch = Chain(pool, s5_step)
        ch.link(nc.gpsimd.memset(m.half[:], -0.5))
        for b in range(NB):
            pool.wait_ge(squared, b + 1)
            root(nc, m, ch, b, D).then_inc(rooted, 1)
        lam = m.lam
        tt, ts = nc.gpsimd.tensor_tensor, nc.gpsimd.tensor_scalar
        pool.wait_ge(lam_act, 1)
        dt = lam[:, 2, 1:2]
        ch.link(ts(lam[:, 3, :], lam[:, 0, :], dt, None, ALU.mult))
        ch.link(ts(lam[:, 4, :], lam[:, 1, :], dt, None, ALU.mult))
        pool.sem_inc(lam_ok, 1)
        MAGIC = 1.5 * 2.0 ** 23
        c1 = 6.28125
        c2 = 2028 / 2.0 ** 20
        c3 = 2 * math.pi - c1 - c2
        ch.link(ts(lam[:, 10, :], lam[:, 4, :], 1.0 / (2 * math.pi), None, ALU.mult))
        ch.link(ts(lam[:, 10, :], lam[:, 10, :], MAGIC, None, ALU.add))
        ch.link(ts(lam[:, 10, :], lam[:, 10, :], MAGIC, None, ALU.subtract))
        src = lam[:, 4, :]
        for c in (c1, c2, c3):
            ch.link(ts(lam[:, 11, :], lam[:, 10, :], c, None, ALU.mult))
            ch.link(tt(lam[:, 6, :], src, lam[:, 11, :], ALU.subtract))
            src = lam[:, 6, :]
        top = 3.1415925
        ch.link(ts(lam[:, 6, :], lam[:, 6, :], top, -top, ALU.min, ALU.max))
        ch.link(ts(lam[:, 11, :], lam[:, 6, :], math.pi / 2, -2 * math.pi, ALU.is_gt, ALU.mult))
        ch.link(ts(lam[:, 7, :], lam[:, 6, :], math.pi / 2, None, ALU.add))
        ch.link(tt(lam[:, 7, :], lam[:, 7, :], lam[:, 11, :], ALU.add))
        ch.link(ts(lam[:, 7, :], lam[:, 7, :], top, -top, ALU.min, ALU.max))
        pool.sem_inc(lam_ok, 1)
        pool.wait_ge(lam_act, 4)
        ch.link(tt(lam[:, 14, :], lam[:, 5, :], lam[:, 9, :], ALU.mult))
        ch.link(tt(lam[:, 15, :], lam[:, 5, :], lam[:, 8, :], ALU.mult))
        ch.link(ts(lam[:, 3, :], lam[:, 14, :], -1.0, None, ALU.add))
        ch.link(tt(lam[:, 6, :], lam[:, 0, :], lam[:, 0, :], ALU.mult))
        ch.link(tt(lam[:, 7, :], lam[:, 1, :], lam[:, 1, :], ALU.mult))
        ch.link(tt(lam[:, 6, :], lam[:, 6, :], lam[:, 7, :], ALU.add))
        pool.sem_inc(lam_ok, 1)
        ch.link(tt(lam[:, 7, :], lam[:, 3, :], lam[:, 0, :], ALU.mult))
        ch.link(tt(lam[:, 8, :], lam[:, 15, :], lam[:, 1, :], ALU.mult))
        ch.link(tt(lam[:, 7, :], lam[:, 7, :], lam[:, 8, :], ALU.add))
        pool.wait_ge(lam_inv, 1)
        ch.link(tt(lam[:, 12, :], lam[:, 7, :], lam[:, 6, :], ALU.mult))
        ch.link(tt(lam[:, 7, :], lam[:, 15, :], lam[:, 0, :], ALU.mult))
        ch.link(tt(lam[:, 8, :], lam[:, 3, :], lam[:, 1, :], ALU.mult))
        ch.link(tt(lam[:, 7, :], lam[:, 7, :], lam[:, 8, :], ALU.subtract))
        ch.link(tt(lam[:, 5, :], lam[:, 7, :], lam[:, 6, :], ALU.mult))
        for dst, s in ((8, 14), (9, 14), (10, 15), (11, 15), (13, 12)):
            ch.link(nc.gpsimd.tensor_copy(lam[:, dst, :], lam[:, s, :]))
        for dst, s in ((14, 5), (15, 5)):
            ch.link(nc.gpsimd.tensor_copy(lam[:, dst, :], lam[:, s, :]))
        pool.sem_inc(prep_ok, 1)
        pool.wait_ge(tr_act, PRM // 2 + 1)
        Pw, F12, G12 = m.Pw, m.F12, m.G12
        ar, ai, zr, zi = (m.prm[:, q, :] for q in range(4))
        ch.link(nc.gpsimd.memset(Pw[:, 0, 0, :], 1.0))
        ch.link(nc.gpsimd.memset(Pw[:, 0, 1, :], 0.0))
        ch.link(nc.gpsimd.tensor_copy(Pw[:, 1, :, :], m.prm[:, 0:2, :]))
        t0, t1 = m.tmp[:, 0, 0:G], m.tmp[:, 1, 0:G]
        for n in range(1, T):
            re, im = Pw[:, n, 0, :], Pw[:, n, 1, :]
            ch.link(tt(t0, re, ar, ALU.mult))
            ch.link(tt(t1, im, ai, ALU.mult))
            ch.link(tt(Pw[:, n + 1, 0, :], t0, t1, ALU.subtract))
            ch.link(tt(t0, re, ai, ALU.mult))
            ch.link(tt(t1, im, ar, ALU.mult))
            ch.link(tt(Pw[:, n + 1, 1, :], t0, t1, ALU.add))
        up, dn = slice(0, ST), slice(ST, P)
        for dst, half, part, sign in ((F12[up, 0], up, 0, 1.0), (F12[dn, 0], dn, 1, -1.0), (F12[up, 1], up, 1, -1.0),
                                      (F12[dn, 1], dn, 0, -1.0)):
            ch.link(ts(dst, Pw[half, :, part, :], sign, None, ALU.mult))
        for dst, half, part, sign in ((G12[up, 0], up, 0, 1.0), (G12[dn, 0], dn, 1, 1.0), (G12[up, 1], up, 1, -1.0),
                                      (G12[dn, 1], dn, 0, 1.0)):
            ch.link(ts(dst, Pw[half, 0:T, part, :], sign, None, ALU.mult))
        ch.link(nc.gpsimd.tensor_copy(m.a8[:, 0, :], Pw[:, T, 0, :]))
        for dst, half, sign in ((m.a8[up, 1], up, 1.0), (m.a8[dn, 1], dn, -1.0), (m.a8[up, 2], up, -1.0), (m.a8[dn, 2], dn, 1.0)):
            ch.link(ts(dst, Pw[half, T, 1, :], sign, None, ALU.mult))
        wide = [P, G, CH]

        def over(v):
            return v.unsqueeze(2).to_broadcast(wide)

        s0, s1 = (m.tmp[:, i, :].rearrange("p (g c) -> p g c", c=CH) for i in range(2))
        pool.wait_ge(b_in, 64)
        Br, Bi = m.Bri[:, 0], m.Bri[:, 1]
        ch.link(tt(s0, Br, over(zr), ALU.mult))
        ch.link(tt(s1, Bi, over(zi), ALU.mult))
        ch.link(tt(m.bb[:, 0], s0, s1, ALU.subtract))
        ch.link(tt(s0, Br, over(zi), ALU.mult))
        ch.link(tt(s1, Bi, over(zr), ALU.mult))
        ch.link(tt(m.bb[:, 1], s0, s1, ALU.add))
        pool.wait_ge(transposed, 16)
        for s in range(T):
            ch.link(tt(s0, m.bb[:, 0], over(G12[:, 0, T - 1 - s, :]), ALU.mult))
            ch.link(tt(s1, m.bb[:, 1], over(G12[:, 1, T - 1 - s, :]), ALU.mult))
            ch.link(tt(m.BT[:, :, s * CH:(s + 1) * CH], s0, s1, ALU.add))
        pool.wait_ge(tr_dve, (CRE + 1) // 2)
        pool.wait_ge(tr_act, (CRE + 1) // 2 + 1)
        Cr, Ci = (m.CrCi[:, r, :].rearrange("p (g c) -> p g c", c=CH) for r in range(2))
        for t in range(T + 1):
            ch.link(tt(s0, Cr, over(F12[:, 0, t, :]), ALU.mult))
            ch.link(tt(s1, Ci, over(F12[:, 1, t, :]), ALU.mult))
            ch.link(tt(m.Cp[:, :, t * CH:(t + 1) * CH], s0, s1, ALU.add))
        for b in range(NB, NB + N_MEM // P):
            pool.wait_ge(squared, b + 1)
            root(nc, m, ch, b, D).then_inc(rooted, 1)


def phase_b(nc, block, m, a, sem):
    U_in, zero_ok, pad_out, k_out, m1_in, bst = (sem(n) for n in ("U_in", "zero_ok", "pad_out", "k_out", "m1_in", "bst"))
    oh_in, line_mm, line_ok, line_out, skewed = (sem(n) for n in ("oh_in", "line_mm", "line_ok", "line_out", "skewed"))
    b_act, b_dve, ones_row = sem("b_act"), sem("b_dve"), sem("ones_row")
    K0, B0, V0, Y0, END = 0, 8, 16, 32, 40
    evac_by = ["dve" if i % 2 or i >= Y0 else "act" for i in range(END)]

    def copied(eng, i):
        eng.wait_ge(b_dve if evac_by[i] == "dve" else b_act, evac_by[:i + 1].count(evac_by[i]))

    @block.sync
    def _(sp):
        sp.wait_ge(line_ok, 3)
        sp.dma_start(a.line_dram, m.line[:]).then_inc(line_out, 16)
        for s in range(T):
            sp.dma_start(m.U[s * CH:(s + 1) * CH], a.u_dram[:, s * J:(s + 1) * J].rearrange("(g c) j -> c g j", c=CH)).then_inc(U_in, 16)
        sp.wait_ge(zero_ok, 1)
        sp.dma_start(a.kp_dram[:, :, 0:112], m.ztile[:]).then_inc(pad_out, 16)
        copied(sp, B0 - 2)
        copied(sp, B0 - 1)
        sp.dma_start(a.kp_dram[:, :, 112:240], m.Krow[:]).then_inc(k_out, 16)
        sp.wait_ge(pad_out, 16)
        sp.wait_ge(k_out, 16)
        for s in range(T):
            sp.dma_start(m.M1[s * CH:(s + 1) * CH], a.kp_dram[:, :, 112 - CH * s:240 - CH * s]).then_inc(m1_in, 16)
        sp.wait_ge(skewed, 16 * H_A)

    def evac(eng, engine, i):
        eng.wait_ge(bst, i + 1)
        bank = m.ps[:, i % 6, :].rearrange("p (g n) -> p g n", g=4)
        done = b_act if evac_by[i] == "act" else b_dve
        copy = (lambda dst, src: nc.scalar.activation(dst, src, ACT.Copy)) if evac_by[i] == "act" else nc.vector.tensor_copy
        if i < B0:
            copy(m.Krow[:, 4 * i:4 * i + 4, :], bank[0:CH]).then_inc(done, 1)
        elif i < V0:
            g = 4 * (i - B0)
            copy(m.Bm[:, g:g + 4, 0:P], bank)
            copy(m.Bm[:, g:g + 4, P:P + ST], bank[:, :, 0:ST]).then_inc(done, 1)
        elif i < Y0:
            if i < V0 + 2:
                eng.wait_ge(k_out, 16)
                eng.wait_ge(pad_out, 16)
            r, q = divmod(i - V0, 8)
            copy(m.V[:, 1:J + 1, r, 4 * q:4 * q + 4], bank.rearrange("p g j -> p j g")).then_inc(done, 1)
        else:
            if i == Y0:
                eng.wait_ge(b_act, evac_by.count("act"))
            for n in range(4):
                g = 4 * (i - Y0) + n
                last = nc.vector.scalar_tensor_tensor(out=m.Y1[:, g, :], in0=m.U[:, g, :], scalar=m.dskip[:, g:g + 1],
                                                      in1=bank[:, n, :], op0=ALU.mult, op1=ALU.add)
            last.then_inc(done, 1)

    @block.scalar
    def _(act):
        act.dma_start(m.ohb[:], a.onehot).then_inc(oh_in, 16)
        act.dma_start(m.rb[0:NUM_BUCKETS], a.rel_bias).then_inc(oh_in, 16)
        act.wait_ge(line_out, 16)
        for h in range(H_A):
            act.dma_start(bass.AP(a.skew_dram.tensor, h * P * (LINE + 1), [[LINE + 1, P], [1, LINE]]),
                          a.line_dram[h:h + 1, :].to_broadcast([P, LINE])).then_inc(skewed, 16)
        for i in range(END):
            if evac_by[i] == "act":
                evac(act, nc.scalar, i)

    @block.vector
    def _(dve):
        for n in range(3):
            dve.wait_ge(line_mm, n + 1)
            nc.vector.tensor_copy(m.line[:, n * 384:(n + 1) * 384], m.ps[0:H_A, 6 + n % 2, 0:384]).then_inc(line_ok, 1)
        dve.wait_ge(U_in, 16 * T)
        for i in range(END):
            if evac_by[i] == "dve":
                evac(dve, nc.vector, i)

    @block.tensor
    def _(pe):
        def group(i, emit):
            if i >= 6:
                copied(pe, i - 6)
            for n in range(4):
                last = emit(n, m.ps[:, i % 6, n * P:(n + 1) * P])
            last.then_inc(bst, 1)

        pe.wait_ge(oh_in, 32)
        pe.wait_ge(ones_row, 1)
        for n in range(3):
            if n == 2:
                pe.wait_ge(line_ok, 1)
            nc.tensor.matmul(m.ps[0:H_A, 6 + n % 2, 0:384], m.rb[:], m.ohb[:, n * 384:(n + 1) * 384],
                             start=True, stop=True).then_inc(line_mm, 1)
        for q in range(8):
            group(K0 + q, lambda n, out: nc.tensor.matmul(out[0:CH], m.BT[:, 4 * q + n, P - CH:P], m.Cp[:, 4 * q + n, 0:P],
                                                          start=True, stop=True))
        for q in range(8):
            group(B0 + q, lambda n, out: nc.tensor.transpose(out, m.BT[:, 4 * q + n, :], m.ident[:]))
        pe.wait_ge(U_in, 16 * T)
        copied(pe, V0 - 1)
        copied(pe, V0 - 2)
        for r in range(2):
            for q in range(8):
                group(V0 + 8 * r + q, lambda n, out: nc.tensor.matmul(out, m.Bm[:, 4 * q + n, ST * r:ST * r + P],
                                                                      m.U[:, 4 * q + n, :], start=True, stop=True))
        pe.wait_ge(m1_in, 16 * T)
        for q in range(8):
            group(Y0 + q, lambda n, out: nc.tensor.matmul(out, m.M1[:, 4 * q + n, :], m.U[:, 4 * q + n, :], start=True, stop=True))

    @block.gpsimd
    def _(pool):
        nc.gpsimd.memset(m.rb[NUM_BUCKETS:ONEHOT_ROWS], 1.0).then_inc(ones_row, 1)
        nc.gpsimd.memset(m.ztile[:], 0.0).then_inc(zero_ok, 1)
        pool.wait_ge(k_out, 16)
        nc.gpsimd.memset(m.V[:, 0], 0.0).then_inc(zero_ok, 1)


def phase_c(nc, block, m, a, sem):
    bias_in = [sem(f"bias_in{h}") for h in range(H_A)]
    scored, maxed, exped, probs_t, probs_copied, valued, normed, c_step, scan_step = (
        sem(n) for n in ("scored", "maxed", "exped", "probs_t", "probs_copied", "valued", "normed", "c_step", "scan_step"))
    tiles = [(h, q) for h in range(H_A) for q in range(NB)]
    N = len(tiles)
    halves = [-(-(q + 1) // 4) for _, q in tiles]
    before = [sum(halves[:i]) for i in range(N + 1)]

    @block.sync
    def _(sp):
        for h in range(H_A):
            src = bass.AP(a.skew_dram.tensor, h * P * (LINE + 1) + P - 1, [[LINE, P], [1, S]])
            sp.dma_start(m.bias[:, h, :], src).then_inc(bias_in[h], 16)

    @block.tensor
    def _(pe):
        def scores(i):
            h, q = tiles[i]
            if i >= 2:
                pe.wait_ge(maxed, i - 1)
            rows = slice(HD_A * (h % 2), HD_A * (h % 2) + HD_A)
            keys = P * (q + 1)
            for lo in range(0, keys, 512):
                n = min(512, keys - lo)
                last = nc.tensor.matmul(m.ps[:, 2 * (i % 2) + lo // 512, 0:n], m.qT[rows, h // 2, q * P:(q + 1) * P],
                                        m.kT[rows, h // 2, lo:lo + n], start=True, stop=True)
            last.then_inc(scored, 1)

        scores(0)
        for i, (h, q) in enumerate(tiles):
            if i + 1 < N:
                scores(i + 1)
            pe.wait_ge(exped, i + 1)
            for n in range(halves[i]):
                g = before[i] + n
                if g >= 2:
                    pe.wait_ge(probs_copied, g - 1)
                for kb in range(4 * n, min(4 * n + 4, q + 1)):
                    last = nc.tensor.transpose(m.ps[:, 4 + g % 2, (kb % 4) * P:(kb % 4 + 1) * P],
                                               m.pr[:, i % 2, kb * P:(kb + 1) * P], m.ident[:])
                last.then_inc(probs_t, 1)
            if i >= 2:
                pe.wait_ge(normed, i - 1)
            for n in range(halves[i]):
                g = before[i] + n
                pe.wait_ge(probs_copied, g + 1)
                for kb in range(4 * n, min(4 * n + 4, q + 1)):
                    last = nc.tensor.matmul(m.ps[:, 6 + i % 2, 0:HD_A], m.prT[:, g % 2, (kb % 4) * P:(kb % 4 + 1) * P],
                                            m.v[:, kb, h * HD_A:(h + 1) * HD_A], start=(kb == 0), stop=(kb == q))
            last.then_inc(valued, 1)

    @block.vector
    def _(dve):
        ch = Chain(dve, c_step)

        def normalise(i):
            h, q = tiles[i]
            dve.wait_ge(valued, i + 1)
            den = m.den[:, i % 4:i % 4 + 1]
            ch.link(nc.vector.reciprocal(den, den))
            nc.vector.tensor_scalar(m.ya[:, q, h * HD_A:(h + 1) * HD_A], m.ps[:, 6 + i % 2, 0:HD_A], den, None,
                                    ALU.mult).then_inc(normed, 1)

        for i, (h, q) in enumerate(tiles):
            if q == 0:
                dve.wait_ge(bias_in[h], 16)
            dve.wait_ge(scored, i + 1)
            if i >= 2:
                dve.wait_ge(exped, i - 1)
            keys = P * (q + 1)
            neg = m.neg[:, i % 4:i % 4 + 1]
            flat = m.ps[:, 2 * (i % 2):2 * (i % 2) + 2, :].rearrange("p b n -> p (b n)")
            ch.link(nc.vector.tensor_tensor_reduce(out=m.sc[:, i % 2, 0:keys], in0=flat[:, 0:keys],
                                                   in1=m.bias[:, h, P * (NB - 1 - q):S], scale=1.0, scalar=-3.0e38,
                                                   op0=ALU.add, op1=ALU.max, accum_out=neg))
            nc.vector.tensor_scalar(neg, neg, -1.0, None, ALU.mult).then_inc(maxed, 1)
            if i:
                normalise(i - 1)
        normalise(N - 1)

    @block.scalar
    def _(act):
        for i, (h, q) in enumerate(tiles):
            keys = P * (q + 1)
            act.wait_ge(maxed, i + 1)
            if i >= 2:
                act.wait_ge(probs_t, before[i - 1])
            if i >= 4:
                act.wait_ge(normed, i - 3)
            nc.scalar.activation(m.pr[:, i % 2, 0:keys], m.sc[:, i % 2, 0:keys], ACT.Exp, bias=m.neg[:, i % 4:i % 4 + 1],
                                 accum_out=m.den[:, i % 4:i % 4 + 1]).then_inc(exped, 1)
            for n in range(halves[i]):
                g = before[i] + n
                act.wait_ge(probs_t, g + 1)
                if g >= 2:
                    owner = max(x for x in range(i + 1) if before[x] <= g - 2)
                    if owner < i:
                        act.wait_ge(valued, owner + 1)
                cols = P * min(4, q + 1 - 4 * n)
                nc.scalar.activation(m.prT[:, g % 2, 0:cols], m.ps[:, 4 + g % 2, 0:cols], ACT.Copy).then_inc(probs_copied, 1)

    @block.gpsimd
    def _(pool):
        t0, t1 = m.scan_t[:, 0], m.scan_t[:, 1]
        tt = nc.gpsimd.tensor_tensor
        re2 = m.a8[:, 0:1, :].to_broadcast([P, 2, G])
        for j in range(J):
            now, nxt = m.V[:, j], m.V[:, j + 1]
            if j:
                pool.wait_ge(scan_step, 5 * j)
            tt(t0, now, re2, ALU.mult).then_inc(scan_step, 1)
            tt(t1, now, m.a8[:, 1:3, :], ALU.mult).then_inc(scan_step, 1)
            pool.wait_ge(scan_step, 5 * j + 2)
            tt(nxt, nxt, t0, ALU.add).then_inc(scan_step, 1)
            pool.wait_ge(scan_step, 5 * j + 3)
            tt(nxt[:, 0], nxt[:, 0], t1[:, 1], ALU.add).then_inc(scan_step, 1)
            tt(nxt[:, 1], nxt[:, 1], t1[:, 0], ALU.add).then_inc(scan_step, 1)


def phase_d(nc, block, m, a, sem):
    wglu_in, wout_in, h_in, yg_out, y_in = sem("wglu_in"), [sem("wout_in0"), sem("wout_in1")], sem("h_in"), sem("yg_out"), sem("y_in")
    wxq_in, wxo_in = sem("wxq_in"), sem("wxo_in")
    filled, d_act, d_dve = sem("filled"), sem("d_act"), sem("d_dve")
    gelued, sq_a, sq_b, sq_h, rooted_d, step_pool, step_dve, step_act = (
        sem(n) for n in ("gelued", "sq_a", "sq_b", "sq_h", "rooted_d", "step_pool", "step_dve", "step_act"))
    gated, scaled_b, h_ready, xn_ready, maxed_x, exped_x, px_ready, y_added = (
        sem(n) for n in ("gated", "scaled_b", "h_ready", "xn_ready", "maxed_x", "exped_x", "px_ready", "y_added"))
    groups, at = [], {}

    def plan(name, count, by):
        at[name] = len(groups)
        groups.extend(by if isinstance(by, list) else [by] * count)

    both = ["act", "dve"]
    plan("Y", 8, "dve")
    plan("YA", 8, both * 4)
    plan("PA", 16, "dve")
    plan("GL", 8, "act")
    plan("SS", 1, "dve")
    plan("PB", 16, "dve")
    plan("HT", 16, both * 8)
    plan("XQ", 8, both * 4)
    for blk in range(9):
        if blk < 8:
            plan(("S", blk), 4, "act")
        if blk:
            plan(("T", blk - 1), 2, both)
            plan(("O", blk - 1), 1, "dve")
    plan("XO", 16, "dve")

    def bank(i):
        return m.ps[:, i % 8, :]

    def copied(eng, i):
        eng.wait_ge(d_dve if groups[i] == "dve" else d_act, groups[:i + 1].count(groups[i]))

    def scaled_copy(who, i, dst, src, g):
        if who == "act":
            nc.scalar.activation(dst, src, ACT.Identity, scale=g).then_inc(d_act, 1)
        else:
            nc.vector.tensor_scalar(dst, src, g, None, ALU.mult).then_inc(d_dve, 1)

    def spread_copy(who, eng, name, i):
        n = at[name] + i
        if groups[n] != who:
            return
        eng.wait_ge(filled, n + 1)
        half, k = divmod(i, 8)
        if name == "YA":
            half, k = divmod(i, 4)
            scaled_copy(who, n, m.yaT[:, k, half * 512:(half + 1) * 512], bank(n), m.g_oa[:, k:k + 1])
        elif name == "HT":
            scaled_copy(who, n, m.hT[:, k, half * 512:(half + 1) * 512], bank(n), m.g_x[:, k:k + 1])
        else:
            c, half = divmod(i, 2)
            scaled_copy(who, n, m.qxT[:, c, half * 512:(half + 1) * 512], bank(n), 1.0)

    blocks = [(hd, half) for hd in range(H_X) for half in range(2)]
    scale_x = HD_X ** -0.5

    @block.sync
    def _(sp):
        sp.dma_start(m.h[:], a.x.rearrange("(b p) d -> p b d", p=P)).then_inc(h_in, 16)
        for n in range(2):
            sp.dma_start((m.wd1, m.wd2)[n][:], chunked(a.w_out, slice(512 * n, 512 * n + 512))).then_inc(wout_in[n], 16)
        sp.dma_start(m.wd0[:, 0:MB], a.w_glu.rearrange("(k p) n -> p k n", p=P)).then_inc(wglu_in, 16)
        sp.wait_ge(gelued, 8)
        for t in range(T):
            sp.dma_start(a.y_dram[:, :, t, :].rearrange("g c j -> c g j"), m.yg[t * CH:(t + 1) * CH]).then_inc(yg_out, 16)
        sp.wait_ge(yg_out, 16 * T)
        sp.dma_start(m.yT[:], a.y_dram.rearrange("(m g) c t j -> (g c) m t j", m=MB)).then_inc(y_in, 16)
        sp.wait_ge(filled, at["SS"])
        sp.dma_start(m.wd0[:], chunked(a.w_xq, slice(0, 512))).then_inc(wxq_in, 16)
        sp.wait_ge(filled, at["HT"])
        sp.dma_start(m.wd1[:].rearrange("p k n -> p (k n)").rearrange("p (k n) -> p k n", k=H_X),
                     a.w_xo.rearrange("(k p) n -> p k n", p=P)).then_inc(wxo_in, 16)

    @block.tensor
    def _(pe):
        count = [0]

        def group(emit):
            i = count[0]
            if i >= 8:
                copied(pe, i - 8)
            emit(bank(i)).then_inc(filled, 1)
            count[0] += 1

        def product(weights, moving, width, kc):
            def emit(out):
                for k in range(kc):
                    last = nc.tensor.matmul(out[:, 0:width], weights(k), moving(k), start=(k == 0), stop=(k == kc - 1))
                return last
            group(emit)

        def transposes(sources):
            def emit(out):
                for n, src in enumerate(sources):
                    last = nc.tensor.transpose(out[:, n * P:(n + 1) * P], src, m.ident[:])
                return last
            group(emit)

        def emit_y(q):
            def emit(out):
                for n in range(4):
                    last = nc.tensor.matmul(out[:, n * P:(n + 1) * P], m.Cp[:, 4 * q + n, CH:CH + P], m.V[:, 0:J, 0, 4 * q + n],
                                            start=True, stop=True)
                return last
            group(emit)

        for q in range(8):
            emit_y(q)
        for half in range(2):
            for k in range(4):
                transposes([m.ya[:, 4 * half + n, k * P:(k + 1) * P] for n in range(4)])
        copied(pe, at["YA"] + 6)
        copied(pe, at["YA"] + 7)
        for n in range(2):
            pe.wait_ge(wout_in[n], 16)
        for b in range(NB):
            for n in range(2):
                product(lambda k: m.yaT[:, k, b * P:(b + 1) * P], lambda k: (m.wd1, m.wd2)[n][:, k, :], 512, 4)
        pe.wait_ge(wglu_in, 16)
        pe.wait_ge(y_in, 16)
        yflat = m.yT[:].rearrange("p m t j -> p m (t j)")
        for c in range(MB):
            for half in range(2):
                product(lambda k: m.wd0[:, k, c * P:(c + 1) * P], lambda k: yflat[:, k, half * 512:(half + 1) * 512], 512, MB)
        pe.wait_ge(sq_b, MB)

        def emit_ss(out):
            for b in range(NB):
                for c in range(MB):
                    last = nc.tensor.matmul(out[:, b:b + 1], m.sq[:, c, b * P:(b + 1) * P], m.ones[:, 0:1], start=(c == 0), stop=(c == MB - 1))
            return last
        group(emit_ss)
        pe.wait_ge(scaled_b, MB)
        for b in range(NB):
            for n in range(2):
                product(lambda k: m.ybT[:, k, b * P:(b + 1) * P], lambda k: (m.wd1, m.wd2)[n][:, 4 + k, :], 512, 4)
        for half in range(2):
            pe.wait_ge(xn_ready, 4 * (half + 1))
            for k in range(KC):
                transposes([(m.xn, m.xnb)[half][:, n, k * P:(k + 1) * P] for n in range(4)])
        copied(pe, at["HT"] + 14)
        copied(pe, at["HT"] + 15)
        pe.wait_ge(wxq_in, 16)
        for c in range(H_X):
            for half in range(2):
                product(lambda k: m.wd0[:, k, c * P:(c + 1) * P], lambda k: m.hT[:, k, half * 512:(half + 1) * 512], 512, KC)
        copied(pe, at["XQ"] + 6)
        copied(pe, at["XQ"] + 7)
        for blk in range(9):
            if blk < 8:
                hd, half = blocks[blk]
                for n in range(4):
                    q = 4 * half + n
                    product(lambda k: m.qxT[:, hd, q * P:(q + 1) * P], lambda k: m.kmT[:, hd, :], N_MEM, 1)
            if blk:
                hd, half = blocks[blk - 1]
                pe.wait_ge(px_ready, 4 * blk)
                for c in range(2):
                    transposes([m.px[:, 4 * ((blk - 1) % 2) + n, c * P:(c + 1) * P] for n in range(4)])
                for c in range(2):
                    copied(pe, at[("T", blk - 1)] + c)
                product(lambda k: m.vm[:, k, hd * P:(hd + 1) * P], lambda k: m.pxT[:, k, :], 512, 2)
        copied(pe, at[("O", 7)])
        pe.wait_ge(wxo_in, 16)
        wxo = m.wd1[:].rearrange("p k n -> p (k n)").rearrange("p (k n) -> p k n", k=H_X)
        for b in range(NB):
            for n in range(2):
                product(lambda k: m.oT[:, k, b * P:(b + 1) * P], lambda k: wxo[:, k, n * 512:(n + 1) * 512], 512, H_X)

    @block.vector
    def _(dve):
        ch = Chain(dve, step_dve)
        for q in range(8):
            n = at["Y"] + q
            dve.wait_ge(filled, n + 1)
            nc.vector.tensor_tensor(m.yg[:, 4 * q:4 * q + 4, :], bank(n).rearrange("p (g j) -> p g j", g=4),
                                    m.Y1[:, 4 * q:4 * q + 4, :], ALU.add).then_inc(d_dve, 1)
        for i in range(8):
            spread_copy("dve", dve, "YA", i)

        def add_to_h(name, i, col):
            b, n = divmod(i, 2)
            dve.wait_ge(filled, at[name] + i + 1)
            out = m.h[:, b, n * 512:(n + 1) * 512]
            if col is None:
                return nc.vector.tensor_tensor(out, out, bank(at[name] + i), ALU.add).then_inc(d_dve, 1)
            return nc.vector.scalar_tensor_tensor(out=out, in0=bank(at[name] + i), scalar=m.rs[:, col + b:col + b + 1], in1=out,
                                                  op0=ALU.mult, op1=ALU.add).then_inc(d_dve, 1)

        dve.wait_ge(h_in, 16)
        dve.wait_ge(rooted_d, 1)
        for i in range(16):
            add_to_h("PA", i, 10)
        dve.wait_ge(y_in, 16)
        for i in range(8):
            c, half = divmod(i, 2)
            copied(dve, at["GL"] + i)
            dst = m.ybT[:, c, :].rearrange("p (j t) -> p t j", t=T)[:, 4 * half:4 * half + 4, :]
            nc.vector.tensor_tensor(dst, m.yT[:, c, 4 * half:4 * half + 4, :],
                                    m.gate_s[:, c, half * 512:(half + 1) * 512].rearrange("p (t j) -> p t j", t=4),
                                    ALU.mult).then_inc(gated, 1)
        for c in range(MB):
            dve.wait_ge(sq_b, c + 1)
            nc.vector.tensor_scalar(m.ybT[:, c, :], m.ybT[:, c, :], m.g_ob[:, c:c + 1], None, ALU.mult).then_inc(scaled_b, 1)
        dve.wait_ge(filled, at["SS"] + 1)
        nc.vector.tensor_copy(m.ss[:, 18:26], bank(at["SS"])[:, 0:NB]).then_inc(d_dve, 1)
        dve.wait_ge(rooted_d, 2)
        copied(dve, at["PA"] + 15)

        def norm(b):
            dve.wait_ge(rooted_d, 3 + b)
            dst = (m.xn, m.xnb)[b // 4][:, b % 4, :]
            nc.vector.tensor_scalar(dst, m.h[:, b], m.rs[:, b:b + 1], None, ALU.mult).then_inc(xn_ready, 1)

        for b in range(NB):
            for n in range(2):
                add_to_h("PB", 2 * b + n, 18)
            if b >= 2:
                norm(b - 2)
        norm(NB - 2)
        norm(NB - 1)
        for i in range(16):
            spread_copy("dve", dve, "HT", i)
        for i in range(8):
            spread_copy("dve", dve, "XQ", i)

        def softmax_front(blk):
            for n in range(4):
                g = at[("S", blk)] + n
                dve.wait_ge(filled, g + 1)
                col = (4 * blk + n) % 8
                neg = m.negx[:, col:col + 1]
                ch.link(nc.vector.reduce_max(neg, bank(g)[:, 0:N_MEM], AX.X))
                nc.vector.tensor_scalar(neg, neg, -scale_x, None, ALU.mult).then_inc(maxed_x, 1)

        def softmax_back(blk):
            for n in range(4):
                i = 4 * blk + n
                dve.wait_ge(exped_x, i + 1)
                den = m.denx[:, i % 8:i % 8 + 1]
                ch.link(nc.vector.reciprocal(den, den))
                px = m.px[:, i % 8, :]
                nc.vector.tensor_scalar(px, px, den, None, ALU.mult).then_inc(px_ready, 1)

        softmax_front(0)
        for blk in range(8):
            softmax_back(blk)
            if blk + 1 < 8:
                softmax_front(blk + 1)
            g = at[("T", blk)] + 1
            dve.wait_ge(filled, g + 1)
            if blk:
                copied(dve, at[("O", blk - 1)])
            nc.vector.tensor_copy(m.pxT[:, 1, :], bank(g)).then_inc(d_dve, 1)
            hd, half = blocks[blk]
            dve.wait_ge(filled, at[("O", blk)] + 1)
            nc.vector.tensor_copy(m.oT[:, hd, half * 512:(half + 1) * 512], bank(at[("O", blk)])).then_inc(d_dve, 1)
        copied(dve, at["PB"] + 15)
        for i in range(16):
            add_to_h("XO", i, None)

    @block.scalar
    def _(act):
        ch = Chain(act, step_act)
        for q in range(8):
            copied(act, at["Y"] + q)
            yg = m.yg[:, 4 * q:4 * q + 4, :]
            nc.scalar.activation(yg, yg, ACT.Gelu).then_inc(gelued, 1)
        for i in range(8):
            spread_copy("act", act, "YA", i)
        for b in range(NB):
            ch.link(nc.scalar.activation(m.junkd[:, 0:D_A], m.ya[:, b], ACT.Square, accum_out=m.ss[:, 10 + b:11 + b]))
        act.sem_inc(sq_a, 1)
        copied(act, at["YA"] + 7)
        for i in range(8):
            c, half = divmod(i, 2)
            act.wait_ge(filled, at["GL"] + i + 1)
            nc.scalar.activation(m.gate_s[:, c, half * 512:(half + 1) * 512], bank(at["GL"] + i), ACT.Sigmoid,
                                 bias=m.bglu[:, c:c + 1]).then_inc(d_act, 1)
        for c in range(MB):
            act.wait_ge(gated, 2 * (c + 1))
            nc.scalar.activation(m.sq[:, c, :], m.ybT[:, c, :], ACT.Square).then_inc(sq_b, 1)
        for b in range(NB):
            copied(act, at["PB"] + 2 * b + 1)
            ch.link(nc.scalar.activation(m.junkd[:], m.h[:, b], ACT.Square, accum_out=m.ss[:, b:b + 1]))
            act.sem_inc(sq_h, 1)
        for i in range(16):
            spread_copy("act", act, "HT", i)
        for i in range(8):
            spread_copy("act", act, "XQ", i)

        def exps(blk):
            for n in range(4):
                i = 4 * blk + n
                act.wait_ge(maxed_x, i + 1)
                if blk >= 2:
                    copied(act, at[("T", blk - 2)] + 1)
                ch.link(nc.scalar.activation(m.px[:, i % 8, :], bank(at[("S", blk)] + n)[:, 0:N_MEM], ACT.Exp, scale=scale_x,
                                             bias=m.negx[:, i % 8:i % 8 + 1], accum_out=m.denx[:, i % 8:i % 8 + 1]))
                act.sem_inc(exped_x, 1)
                act.sem_inc(d_act, 1)

        exps(0)
        for blk in range(8):
            if blk + 1 < 8:
                exps(blk + 1)
            g = at[("T", blk)]
            act.wait_ge(filled, g + 1)
            if blk:
                copied(act, at[("O", blk - 1)])
            nc.scalar.activation(m.pxT[:, 0, :], bank(g), ACT.Copy).then_inc(d_act, 1)

    @block.gpsimd
    def _(pool):
        ch = Chain(pool, step_pool)
        pool.wait_ge(sq_a, 1)
        root(nc, m, ch, 10, D_A, NB).then_inc(rooted_d, 1)
        copied(pool, at["SS"])
        root(nc, m, ch, 18, D_B, NB).then_inc(rooted_d, 1)
        for b in range(NB):
            pool.wait_ge(sq_h, b + 1)
            root(nc, m, ch, b, D).then_inc(rooted_d, 1)


def phase_e(nc, block, m, a, sem):
    wr_in, acc_out, xn_out = sem("wr_in"), sem("acc_out"), sem("xn_out")
    sq3, root3, xn3, step_pool, step_dve, step_act = (sem(n) for n in ("sq3", "root3", "xn3", "step_pool_e", "step_dve_e", "step_act_e"))
    filled, e_act, e_dve = sem("filled_e"), sem("e_act"), sem("e_dve")
    consts, diffed, exped, mask_ok, onehots, gates_ok = (sem(n) for n in ("consts", "diffed", "exped_e", "mask_ok", "onehots", "gates_ok"))
    HT, LG, RK, LS = 0, 16, 17, 19
    PAIRS = NB * TOPK

    def copied(eng, i):
        if i < HT + 16:
            eng.wait_ge(e_act if i % 2 == 0 else e_dve, i // 2 + 1)
        else:
            eng.wait_ge(e_dve, 8 + i - LG + 1)

    def bank(i):
        return m.ps[:, i % 8, :]

    @block.sync
    def _(sp):
        sp.dma_start(a.acc_dram[0:S].rearrange("(b p) d -> p b d", p=P), m.h[:]).then_inc(acc_out, 16)
        sp.dma_start(a.acc_dram[S:S + WIN].rearrange("(b p) d -> p b d", p=P), m.h[:, 0:WIN // P]).then_inc(acc_out, 16)
        for half in range(2):
            sp.wait_ge(xn3, 4 * (half + 1))
            sp.dma_start(a.xn_dram[512 * half:512 * half + 512].rearrange("(b p) d -> p b d", p=P), (m.xn, m.xnb)[half][:]).then_inc(xn_out, 16)
        sp.wait_ge(acc_out, 32)
        sp.wait_ge(xn_out, 32)

    @block.scalar
    def _(act):
        ch = Chain(act, step_act)
        act.dma_start(m.wr[:], a.w_router.rearrange("(k p) n -> p k n", p=P)).then_inc(wr_in, 16)
        act.dma_start(m.br[:], a.b_router.rearrange("(a n) -> a n", a=1)).then_inc(wr_in, 16)
        for b in range(NB):
            ch.link(nc.scalar.activation(m.junkd[:], m.h[:, b], ACT.Square, accum_out=m.ss[:, b:b + 1]))
            act.sem_inc(sq3, 1)
        for i in range(0, 16, 2):
            half, k = divmod(i, 8)
            act.wait_ge(filled, i + 1)
            nc.scalar.activation(m.hT[:, k, half * 512:(half + 1) * 512], bank(i), ACT.Identity, scale=m.g_moe[:, k:k + 1]).then_inc(e_act, 1)
        act.wait_ge(diffed, 1)
        nc.scalar.activation(m.gates[:, :, 0:TOPK], m.gates[:, :, 0:TOPK], ACT.Exp).then_inc(exped, 1)

    @block.tensor
    def _(pe):
        for half in range(2):
            pe.wait_ge(xn3, 4 * (half + 1))
            for k in range(KC):
                i = 8 * half + k
                if i >= 8:
                    copied(pe, i - 8)
                for n in range(4):
                    last = nc.tensor.transpose(bank(i)[:, n * P:(n + 1) * P], (m.xn, m.xnb)[half][:, n, k * P:(k + 1) * P], m.ident[:])
                last.then_inc(filled, 1)
        pe.wait_ge(e_act, 8)
        pe.wait_ge(e_dve, 8)
        pe.wait_ge(wr_in, 32)
        for b in range(NB):
            out = bank(LG)[:, b * E:(b + 1) * E]
            for k in range(KC):
                nc.tensor.matmul(out, m.hT[:, k, b * P:(b + 1) * P], m.wr[:, k, :], start=(k == 0), stop=False)
            last = nc.tensor.matmul(out, m.ones[0:1, :], m.br[:], start=False, stop=True)
        last.then_inc(filled, 1)
        pe.wait_ge(mask_ok, 1)
        pe.wait_ge(consts, 4)
        mask = m.maskE[:].rearrange("p b e -> p (b e)")
        nc.tensor.matmul(bank(RK)[:, 0:NB * E], m.tri[:], mask, start=True, stop=True).then_inc(filled, 1)
        nc.tensor.matmul(bank(RK + 1)[:, 0:NB * E], m.ones[:], mask, start=True, stop=True).then_inc(filled, 1)
        for n in range(PAIRS):
            pe.wait_ge(onehots, 3 * (n + 1))
            nc.tensor.matmul(bank(LS), m.lo[:, n % 4, :], m.hi[:, n % 4].rearrange("p a w -> p (a w)"),
                             start=(n == 0), stop=(n == PAIRS - 1)).then_inc(filled, 1)

    @block.vector
    def _(dve):
        ch = Chain(dve, step_dve)
        v = nc.vector
        for b in range(NB):
            dve.wait_ge(root3, b + 1)
            dst = (m.xn, m.xnb)[b // 4][:, b % 4, :]
            v.tensor_scalar(dst, m.h[:, b], m.rs[:, b:b + 1], None, ALU.mult).then_inc(xn3, 1)
        for i in range(1, 16, 2):
            half, k = divmod(i, 8)
            dve.wait_ge(filled, i + 1)
            v.tensor_scalar(m.hT[:, k, half * 512:(half + 1) * 512], bank(i), m.g_moe[:, k:k + 1], None, ALU.mult).then_inc(e_dve, 1)
        dve.wait_ge(filled, LG + 1)
        v.tensor_copy(m.logit[:].rearrange("p b e -> p (b e)"), bank(LG)[:, 0:NB * E]).then_inc(e_dve, 1)
        dve.wait_ge(e_dve, 9)
        for b in range(NB):
            last = v.max(m.top8[:, b, :], m.logit[:, b, :])
            ch.step(last)
        dve.wait_ge(ch.sem, ch.n)
        for b in range(NB):
            ch.step(v.max_index(m.idx8[:, b, :], m.top8[:, b, :], m.logit[:, b, :]))
        v.tensor_tensor(m.gates[:, :, 0:TOPK], m.top8[:, :, 0:TOPK], m.top8[:, :, 0:1].to_broadcast([P, NB, TOPK]),
                        ALU.subtract).then_inc(diffed, 1)
        dve.wait_ge(ch.sem, ch.n)
        ch.link(v.tensor_copy(m.idxf[:], m.idx8[:]))
        four = [P, NB, TOPK, E]
        dve.wait_ge(consts, 4)
        for k in range(TOPK):
            ch.step(v.tensor_tensor(m.m4[:, :, k, :], m.idxf[:, :, k:k + 1].to_broadcast([P, NB, E]),
                                    m.iota_e[:].unsqueeze(1).to_broadcast([P, NB, E]), ALU.is_equal))
        dve.wait_ge(ch.sem, ch.n)
        v.reduce_sum(m.maskE[:], m.m4[:].rearrange("p b k e -> p b e k"), AX.X).then_inc(mask_ok, 1)
        dve.wait_ge(exped, 1)
        ch.link(v.reduce_sum(m.gsum[:, 0, :], m.gates[:, :, 0:TOPK], AX.X))
        ch.link(v.reciprocal(m.gsum[:, 1, :], m.gsum[:, 0, :]))
        ch.link(v.tensor_tensor(m.gates[:, :, 0:TOPK], m.gates[:, :, 0:TOPK],
                                m.gsum[:, 1, :].unsqueeze(2).to_broadcast([P, NB, TOPK]), ALU.mult))
        dve.wait_ge(filled, RK + 2)
        ch.link(v.memset(m.pref[:, 0, :], 0.0))
        for b in range(NB):
            ch.link(v.tensor_tensor(m.pref[:, b + 1, :], m.pref[:, b, :], bank(RK + 1)[:, b * E:(b + 1) * E], ALU.add))
        ch.link(v.tensor_tensor(m.rank[:].rearrange("p b e -> p (b e)"), bank(RK)[:, 0:NB * E],
                                m.pref[:, 0:NB, :].rearrange("p b e -> p (b e)"), ALU.add))
        ch.link(v.tensor_copy(m.cnt_i[:], m.pref[0:1, NB, :]))
        dve.sem_inc(e_dve, 2)
        for k in range(TOPK):
            ch.step(v.tensor_tensor(m.m4[:, :, k, :], m.m4[:, :, k, :], m.rank[:], ALU.mult))
        dve.wait_ge(ch.sem, ch.n)
        rk, lof, hif = m.dest[:, 0], m.dest[:, 1], m.dest[:, 2]
        ch.link(v.reduce_sum(rk.rearrange("p (b k) -> p b k", k=TOPK), m.m4[:], AX.X))
        ri, li = m.desti[:, 0], m.desti[:, 1]
        ch.link(v.tensor_copy(ri, rk))
        ch.link(v.tensor_scalar(li, ri, P - 1, None, ALU.bitwise_and))
        ch.link(v.tensor_copy(lof, li))
        ch.link(v.tensor_tensor(rk, rk, lof, ALU.subtract))
        ch.link(v.tensor_scalar(rk, rk, 1.0 / P, None, ALU.mult))
        ch.link(v.scalar_tensor_tensor(out=hif.rearrange("p (b k) -> p b k", k=TOPK), in0=m.idxf[:, :, 0:TOPK], scalar=float(S // P),
                                       in1=rk.rearrange("p (b k) -> p b k", k=TOPK), op0=ALU.mult, op1=ALU.add))
        dve.wait_ge(xn_out, 32)
        for n in range(PAIRS):
            if n >= 4:
                dve.wait_ge(filled, RK + 2 + n - 3)
            b, k = divmod(n, TOPK)
            v.tensor_scalar(m.lo[:, n % 4, :], m.iota_w[:, 0:P], lof[:, n:n + 1], None, ALU.is_equal).then_inc(onehots, 1)
            v.tensor_scalar(m.hi[:, n % 4, 0, :], m.iota_w[:], hif[:, n:n + 1], m.tok1[:, b:b + 1], ALU.is_equal, ALU.mult).then_inc(onehots, 1)
            v.tensor_scalar(m.hi[:, n % 4, 1, :], m.iota_w[:], hif[:, n:n + 1], m.gates[:, b, k:k + 1], ALU.is_equal, ALU.mult).then_inc(onehots, 1)
        dve.wait_ge(filled, LS + PAIRS)
        ch.link(v.tensor_copy(m.list_f[:].rearrange("p a w -> p (a w)"), bank(LS)))
        tok, empty = m.list_f[:, 0], m.list_t[:, 0]
        ch.link(v.tensor_copy(m.gate_l[:], m.list_f[:, 1]))
        ch.link(v.tensor_scalar(empty, tok, 0.0, None, ALU.is_equal))
        ch.link(v.scalar_tensor_tensor(out=m.list_t[:, 1], in0=empty, scalar=4096.0, in1=tok, op0=ALU.mult, op1=ALU.add))
        ch.link(v.tensor_scalar(m.idx_g[:], m.list_t[:, 1], -1.0, None, ALU.add))
        ch.link(v.tensor_tensor(empty, empty, m.dumpid[:], ALU.mult))
        ch.link(v.tensor_tensor(empty, empty, tok, ALU.add))
        ch.link(v.tensor_scalar(m.idx_s[:], empty, -1.0, None, ALU.add))

    @block.gpsimd
    def _(pool):
        ch = Chain(pool, step_pool)
        g = nc.gpsimd
        g.memset(m.tri[:], 1.0).then_inc(consts, 1)
        g.iota(m.iota_e[:], [[1, E]], base=0, channel_multiplier=0, allow_small_or_imprecise_dtypes=True)
        g.iota(m.iota_w[:], [[1, WIN]], base=0, channel_multiplier=0, allow_small_or_imprecise_dtypes=True).then_inc(consts, 1)
        g.iota(m.tok1[:], [[P, NB]], base=1, channel_multiplier=1, allow_small_or_imprecise_dtypes=True)
        g.iota(m.dumpid[:], [[0, WIN // 2], [P, 2]], base=DUMP + 1, channel_multiplier=1, allow_small_or_imprecise_dtypes=True).then_inc(consts, 1)
        pool.wait_ge(consts, 1)
        g.affine_select(out=m.tri[:], in_=m.tri[:], compare_op=ALU.is_gt, fill=0.0, base=0, pattern=[[1, P]],
                        channel_multiplier=-1).then_inc(consts, 1)
        for b in range(NB):
            pool.wait_ge(sq3, b + 1)
            root(nc, m, ch, b, D).then_inc(root3, 1)


def each_task(eng, m, name, body):
    done, count = eng.alloc_register(f"tasks_{name}"), eng.alloc_register(f"count_{name}")
    eng.reg_mov(done, 0)
    with eng.Fori(0, E) as e:
        eng.reg_load(count, m.cnt_i[0:1, bass.ds(e, 1)])
        with eng.Fori(0, NWIN) as w:
            left = eng.snap(eng.snap(count, min_val=0, max_val=S) - w * WIN)
            with eng.If(left > 0):
                body(e, w, eng.snap(done, min_val=0, max_val=E * NWIN), left)
                eng.reg_add(done, done, 1)
    return done


def phase_f(nc, block, m, a, sem):
    L1S, SLOTS = 8, 12
    w_in = [sem(f"we_in{s}") for s in range(SLOTS)]
    gathered, scattered = [sem("gathered0"), sem("gathered1")], [sem("scattered0"), sem("scattered1")]
    x_full, xt_act, xt_dve, l1_full, fronted, swished, acted = (
        sem(n) for n in ("x_full", "xt_act", "xt_dve", "l1_full", "fronted", "swished", "acted"))
    l2_full, biased, o_full, o_ready, step_f, init_f, idx_step = (
        sem(n) for n in ("l2_full", "biased", "o_full", "o_ready", "step_f", "init_f", "idx_step"))
    psum_init, rows_in, rows_out, pool_seen = sem("psum_init"), sem("rows_in"), sem("rows_out"), sem("pool_seen")
    JF = F // P

    @block.sync
    def _(sp):
        def body(e, w, n, left):
            for s in range(SLOTS):
                if s < L1S:
                    lo = F * (s % 2) + WIN * (s // 2)
                    src = a.w1[bass.ds(e, 1), :, lo:lo + WIN]
                    sp.wait_ge(l1_full, n * JF + 2 * (s // 2) + 2)
                else:
                    lo = WIN * (s - L1S)
                    src = a.w2[bass.ds(e, 1), :, lo:lo + WIN]
                    sp.wait_ge(l2_full, n * KC + 2 * (s - L1S) + 2)
                sp.dma_start(m.we[s][:], src.rearrange("o (k p) n -> p (o k) n", p=P)).then_inc(w_in[s], 16)

        each_task(sp, m, "sp", body)

    @block.gpsimd
    def _(pool):
        g = nc.gpsimd
        for buf in (m.xg0, m.xg1, m.orow0, m.orow1):
            g.memset(buf[:], 0.0).then_inc(init_f, 1)
        g.iota(m.sx[:], [[P, 2]], base=DUMP, channel_multiplier=1).then_inc(init_f, 1)
        pool.wait_ge(init_f, 5)
        before, gathers1, scatters1 = (pool.alloc_register(r) for r in ("left_before", "gathers1", "scatters1"))
        for r in (before, gathers1, scatters1):
            pool.reg_mov(r, 0)
        xg, orow = (m.xg0, m.xg1), (m.orow0, m.orow1)
        last_row, last_token = pool.to_reg(S + WIN - 1), pool.to_reg(S - 1)

        def value(r, top):
            return pool.snap(r, min_val=0, max_val=top)

        def scatter(half):
            pool.indirect_dma_start(a.acc_dram, bass.IndirectOffsetOnAxis(m.sx[:, half:half + 1], 0), orow[half][:], None,
                                    bounds_check=last_row, oob_is_err=True, compute_op=ALU.add).then_inc(scattered[half], 16)

        def scatter_last(n):
            pool.wait_ge(o_ready, n * 4 + 1)
            pool.sem_inc(pool_seen, 1)
            scatter(0)
            with pool.If(value(before, S) > P):
                scatter(1)
                pool.wait_ge(scattered[1], value(scatters1, E * NWIN) * 16 + 16)
                pool.reg_add(scatters1, scatters1, 1)
            pool.wait_ge(scattered[0], n * 16 + 16)
            pool.sem_inc(rows_out, 1)

        def gather(half):
            pool.indirect_dma_start(xg[half][:], None, a.xn_dram, bass.IndirectOffsetOnAxis(m.gx[:, half:half + 1], 0),
                                    bounds_check=last_token, oob_is_err=False).then_inc(gathered[half], 16)

        def body(e, w, n, left):
            pool.wait_ge(x_full, n * 4 + 1)
            g.tensor_copy(m.gx[:], m.idx_g[:, bass.ds(e * 8 + w * 2, 2)]).then_inc(idx_step, 1)
            pool.wait_ge(idx_step, n * 2 + 1)
            pool.sem_inc(pool_seen, 1)
            gather(0)
            with pool.If(left > P):
                gather(1)
                pool.wait_ge(gathered[1], value(gathers1, E * NWIN) * 16 + 16)
                pool.reg_add(gathers1, gathers1, 1)
            pool.wait_ge(gathered[0], n * 16 + 16)
            pool.sem_inc(rows_in, 1)
            scatter_last(n)
            g.tensor_copy(m.sx[:], m.idx_s[:, bass.ds(e * 8 + w * 2, 2)]).then_inc(idx_step, 1)
            pool.reg_mov(before, left)
            pool.wait_ge(idx_step, n * 2 + 2)

        done = each_task(pool, m, "pool", body)
        scatter_last(pool.snap(done, min_val=0, max_val=E * NWIN))

    @block.tensor
    def _(pe):
        pe.sem_inc(l1_full, JF)
        pe.sem_inc(l2_full, KC)
        pe.sem_inc(x_full, 1)
        pe.wait_ge(init_f, 5)
        pe.wait_ge(psum_init, 1)

        def products(n, W):
            for j in range(JF):
                bank = m.ps[:, 2 + j % 3, :]
                if j % 2 == 0:
                    pe.wait_ge(w_in[j], n * 16 + 16)
                    pe.wait_ge(w_in[j + 1], n * 16 + 16)
                if j >= 3:
                    pe.wait_ge(acted, n * JF + j - 1)
                for part in range(2):
                    slot = m.we[2 * (j // 2) + part]
                    for k in range(KC):
                        last = nc.tensor.matmul(bank[:, part * WIN:part * WIN + W], slot[:, k, (j % 2) * P:(j % 2 + 1) * P],
                                                m.xT[:, k, 0:W], start=(k == 0), stop=(k == KC - 1))
                last.then_inc(l1_full, 1)
            pe.wait_ge(acted, n * JF + JF + 1)
            for j in range(KC):
                slot = m.we[L1S + j // 2]
                if j % 2 == 0:
                    pe.wait_ge(w_in[L1S + j // 2], n * 16 + 16)
                if j >= 2:
                    pe.wait_ge(biased, n * KC + j - 1)
                for k in range(JF):
                    last = nc.tensor.matmul(m.ps[:, 5 + j % 2, 0:W], slot[:, k, (j % 2) * P:(j % 2 + 1) * P], m.act[:, k, 0:W],
                                            start=(k == 0), stop=(k == JF - 1))
                last.then_inc(l2_full, 1)

        def body(e, w, n, left):
            pe.wait_ge(rows_in, n + 1)
            for q in range(4):
                if q < 2:
                    pe.wait_ge(o_ready, n * 4 + 1)
                else:
                    pe.wait_ge((xt_act, xt_dve)[q % 2], n * 4 + 2)
                for i in range(2):
                    for half, xg in enumerate((m.xg0, m.xg1)):
                        k = 2 * q + i
                        last = nc.tensor.transpose(m.ps[:, q % 2, WIN * i + P * half:WIN * i + P * half + P], xg[:, k * P:(k + 1) * P], m.ident[:])
                last.then_inc(x_full, 1)
            pe.wait_ge(xt_act, n * 4 + 4)
            pe.wait_ge(xt_dve, n * 4 + 4)
            for c, W in enumerate(WIDTHS):
                kind = pe.snap((left + (S - 1)) >> 6) - S // 64
                with pe.If(kind == c) if W < WIN else pe.If(kind > c - 1):
                    products(n, W)
            for half in range(2):
                for q in range(2):
                    o = 2 * half + q
                    pe.wait_ge(biased, n * KC + 4 * q + 4)
                    if o >= 2:
                        pe.wait_ge(o_ready, n * 4 + o)
                    for i in range(4):
                        last = nc.tensor.transpose(m.ps[:, o % 2, P * i:P * i + P], m.outT[:, 4 * q + i, half * P:half * P + P], m.ident[:])
                    last.then_inc(o_full, 1)

        each_task(pe, m, "pe", body)

    @block.vector
    def _(dve):
        v = nc.vector
        v.memset(m.ps[:, 2:7, :], 0.0).then_inc(psum_init, 1)
        dve.sem_inc(acted, 1)
        dve.sem_inc(o_ready, 1)
        STEPS = 3 * JF

        def front(e, n, j):
            bank, b = m.ps[:, 2 + j % 3, :], j % 2
            dve.wait_ge(l1_full, n * JF + JF + j + 1)
            dve.wait_ge(acted, n * JF + max(j, 1))
            v.tensor_scalar(m.xlin[:, b, 0, :], bank[:, 0:WIN], m.b1T[:, bass.ds(e * 16 + j, 1)], LIMIT, ALU.add, ALU.min).then_inc(fronted, 1)
            v.tensor_scalar(m.xlin[:, b, 1, :], bank[:, WIN:2 * WIN], m.b1T[:, bass.ds(e * 16 + JF + j, 1)], LIMIT, ALU.add, ALU.min).then_inc(step_f, 1)
            dve.wait_ge(step_f, n * STEPS + steps(j) + 1)
            v.tensor_scalar(m.xlin[:, b, 1, :], m.xlin[:, b, 1, :], -LIMIT, 1.0, ALU.max, ALU.add).then_inc(step_f, 1)

        def steps(j):
            return 2 * j + max(j - 1, 0)

        def back(n, j):
            b = j % 2
            dve.wait_ge(swished, n * JF + j + 1)
            v.tensor_tensor(m.sg[:, b, :], m.sg[:, b, :], m.xlin[:, b, 0, :], ALU.mult).then_inc(step_f, 1)
            at = steps(j + 1) + 3 if j + 1 < JF else STEPS
            dve.wait_ge(step_f, n * STEPS + at)
            v.tensor_tensor(m.act[:, j, :], m.sg[:, b, :], m.xlin[:, b, 1, :], ALU.mult).then_inc(acted, 1)

        def body(e, w, n, left):
            for q in (1, 3):
                dve.wait_ge(x_full, n * 4 + q + 2)
                for i in range(2):
                    k = 2 * q + i
                    v.tensor_scalar(m.xT[:, k, :], m.ps[:, 1, WIN * i:WIN * i + WIN], m.g_moe[:, k:k + 1], None, ALU.mult).then_inc(xt_dve, 1)
            for j in range(JF):
                front(e, n, j)
                if j:
                    back(n, j - 1)
            back(n, JF - 1)
            for j in range(KC):
                dve.wait_ge(l2_full, n * KC + KC + j + 1)
                v.tensor_scalar(m.outT[:, j, :], m.ps[:, 5 + j % 2, 0:WIN], m.b2T[:, bass.ds(e * KC + j, 1)], None, ALU.add).then_inc(biased, 1)
            for o in range(4):
                half, q = divmod(o, 2)
                dve.wait_ge(o_full, n * 4 + o + 1)
                if o == 0:
                    dve.wait_ge(rows_out, n + 1)
                v.tensor_scalar((m.orow0, m.orow1)[half][:, q * 512:(q + 1) * 512], m.ps[:, o % 2, :],
                                m.gate_l[:, bass.ds(e * 8 + w * 2 + half, 1)], None, ALU.mult).then_inc(o_ready, 1)

        each_task(dve, m, "dve", body)

    @block.scalar
    def _(act):
        def body(e, w, n, left):
            for q in (0, 2):
                act.wait_ge(x_full, n * 4 + q + 2)
                for i in range(2):
                    k = 2 * q + i
                    nc.scalar.activation(m.xT[:, k, :], m.ps[:, 0, WIN * i:WIN * i + WIN], ACT.Identity,
                                         scale=m.g_moe[:, k:k + 1]).then_inc(xt_act, 1)
            for j in range(JF):
                act.wait_ge(fronted, n * JF + j + 1)
                act.wait_ge(acted, n * JF + max(j, 1))
                nc.scalar.activation(m.sg[:, j % 2, :], m.xlin[:, j % 2, 0, :], ACT.Sigmoid, scale=ALPHA).then_inc(swished, 1)

        each_task(act, m, "act", body)


def phase_g(nc, block, m, a, sem):
    f_in, f_out, g_in = [sem(f"f_in{b}") for b in range(NB)], sem("f_out"), sem("g_in")
    sq_f, root_f, fin_ok, step_g, act_g = (sem(n) for n in ("sq_f", "root_f", "fin_ok", "step_g", "act_g"))

    @block.sync
    def _(sp):
        for b in range(NB):
            sp.dma_start(m.fin[:, b], a.acc_dram[b * P:(b + 1) * P]).then_inc(f_in[b], 16)
        for b in range(NB):
            sp.wait_ge(fin_ok, b + 1)
            sp.dma_start(a.out[0, b * P:(b + 1) * P], m.fout[:, b]).then_inc(f_out, 16)
        sp.wait_ge(f_out, 16 * NB)

    @block.scalar
    def _(act):
        ch = Chain(act, act_g)
        act.dma_start(m.gfin[:], a.norm_final.rearrange("(a n) -> a n", a=1).to_broadcast([P, D])).then_inc(g_in, 16)
        for b in range(NB):
            act.wait_ge(f_in[b], 16)
            ch.link(nc.scalar.activation(m.jf[:], m.fin[:, b], ACT.Square, accum_out=m.ss[:, b:b + 1]))
            act.sem_inc(sq_f, 1)

    @block.gpsimd
    def _(pool):
        ch = Chain(pool, step_g)
        for b in range(NB):
            pool.wait_ge(sq_f, b + 1)
            root(nc, m, ch, b, D).then_inc(root_f, 1)

    @block.vector
    def _(dve):
        dve.wait_ge(g_in, 16)
        for b in range(NB):
            dve.wait_ge(root_f, b + 1)
            nc.vector.scalar_tensor_tensor(out=m.fout[:, b], in0=m.fin[:, b], scalar=m.rs[:, b:b + 1], in1=m.gfin[:],
                                           op0=ALU.mult, op1=ALU.mult).then_inc(fin_ok, 1)


_SCRATCH = {"u_dram": (D_B, S), "kp_dram": (CH, G, 240), "line_dram": (H_A, LINE), "skew_dram": (H_A, P, LINE + 1), "y_dram": (G, CH, T, J),
            "xn_dram": (S, D), "acc_dram": (S + WIN, D)}


def hybrid_trunk_kernel(nc, aps):
    aps = dict(aps, **{name: nc.dram_tensor(name, shape, F32).ap() for name, shape in _SCRATCH.items()})
    a = namedtuple("Arrays", aps)(**aps)
    with ExitStack() as ctx:
        ctx.enter_context(nc.allow_non_contiguous_dma(reason="gains and parameters stand by column, a few KB in all"))
        m = memory(nc, ctx)

        for phase in PHASES:
            held = []

            def sem(name):
                held.append(nc.alloc_semaphore(name=name))
                return held[-1]

            with nc.Block() as block:
                phase(nc, block, m, a, sem)
            nc.clear_and_free_semaphores(held)
            nc.all_engine_barrier()


PHASES = [phase_a, phase_b, phase_c, phase_d, phase_e, phase_f, phase_g]

_STACKED = ("norm_mix", "w_in", "s5_a_re", "s5_a_im", "s5_b_re", "s5_b_im", "s5_c_re", "s5_c_im", "s5_log_dt", "s5_d",
            "w_glu", "b_glu", "g_out_attn", "g_out_ssm", "w_out", "norm_xattn", "norm_mem", "w_xq", "w_xkv", "w_xo",
            "norm_moe", "w_router", "b_router", "w1", "b1", "w2", "b2", "x", "mem")
_INS = _STACKED + ("rel_bias", "norm_final")


def kernel(**inputs):
    import numpy as _np
    import concourse.bacc as _bacc
    from concourse import mybir as _mybir
    from concourse.bass_utils import run_bass_kernel_spmd as _run

    nc = _bacc.Bacc("TRN2", target_bir_lowering=False, num_devices=1)
    arrays, aps = {}, {}
    for name in _INS:
        arr = _np.ascontiguousarray(inputs[name])
        arrays[f"in_{name}"] = arr
        ap = nc.dram_tensor(f"in_{name}", arr.shape, _mybir.dt.from_np(arr.dtype), kind="ExternalInput").ap()
        aps[name] = ap[0] if name in _STACKED else ap
    arrays["in_onehot"] = shape_constants()
    aps["onehot"] = nc.dram_tensor("in_onehot", (ONEHOT_ROWS, LINE), F32, kind="ExternalInput").ap()
    aps["out"] = nc.dram_tensor("out_0", (1, S, D), F32, kind="ExternalOutput").ap()
    hybrid_trunk_kernel(nc, aps)
    r = _run(nc, [arrays], core_ids=[0])
    return r.results[0]["out_0"]
```

```python
import math
from collections import namedtuple
from contextlib import ExitStack

import numpy as np

import concourse.bass as bass
from concourse import mybir

F32 = mybir.dt.float32
I32 = mybir.dt.int32
U32 = mybir.dt.uint32
ACT = mybir.ActivationFunctionType
ALU = mybir.AluOpType
AX = mybir.AxisListType

P = 128
D = 1024
S = 1024
NB = S // P
KC = D // P
EPS = 1e-5
NEG = -1e30
H_A, HD_A = 8, 64
D_A = H_A * HD_A
WIN_DIL = ((128, 1), (512, 4), (2048, 16))
NUM_BUCKETS, REL_MAX = 32, 2048
D_B = D - D_A
MB = D_B // P
CH = 16
G = D_B // CH
ST = 64
T = 8
J = S // T
N_MEM, H_X, HD_X = 256, 4, 128
E, TOPK, F = 32, 4, 1024
LIMIT, ALPHA = 7.0, 1.702
LINE = 1152
WIN = 256
NWIN = S // WIN
STEP = 8
WIDTHS = tuple(range(P, WIN + 1, STEP))
L1S, SLOTS = 8, 12
DUMP = S
KB = 1024
BASE = 16640

ONEHOT_ROWS = NUM_BUCKETS + 1


def shape_constants():
    dist = S - 1 - np.arange(LINE)
    n = np.maximum(dist, 0)
    exact = NUM_BUCKETS // 2
    nf = np.maximum(n, 1).astype(np.float32)
    scale = np.float32(math.log(REL_MAX / exact))
    large = exact + (np.log(nf / np.float32(exact)) / scale * np.float32(NUM_BUCKETS - exact)).astype(np.int32)
    bucket = np.where(n < exact, n, np.minimum(large, NUM_BUCKETS - 1))
    held = sum(((dist % d == 0) & (dist >= 0) & (dist <= w)).astype(np.float64) for w, d in WIN_DIL)
    table = np.zeros((ONEHOT_ROWS, LINE), np.float32)
    table[bucket, np.arange(LINE)] = 1.0
    table[NUM_BUCKETS] = np.where(held > 0, np.log(np.maximum(held, 1)), NEG)
    return table


class Chain:

    def __init__(self, eng, sem):
        self.eng, self.sem, self.n = eng, sem, 0

    def step(self, ins):
        self.n += 1
        ins.then_inc(self.sem, 1)
        return self.n

    def link(self, ins):
        self.eng.wait_ge(self.sem, self.step(ins))


def memory(nc, ctx):
    m = {}

    def at(name, kib, shape, dt=F32):
        t = nc.alloc_sbuf_tensor_at(name, shape, dt, offset=BASE + int(kib * KB))
        m[name] = t
        return t

    at("qT", 0, [P, D_A // P, S])
    at("kT", 16, [P, D_A // P, S])
    at("v", 32, [P, NB, D_A])
    at("uT", 0, [P, MB, S])
    at("kmT", 48, [P, H_X, N_MEM])
    at("vm", 52, [P, N_MEM // P, H_X * HD_X])
    off = [56 * KB]

    def small(name, shape, dt=F32):
        t = nc.alloc_sbuf_tensor_at(name, shape, dt, offset=BASE + off[0])
        off[0] += -(-(int(np.prod(shape[1:])) * 4) // 32) * 32
        assert off[0] <= 64 * KB, name
        m[name] = t

    small("ident", [P, P])
    small("b1T", [P, E * 16])
    small("b2T", [P, E * KC])
    small("g_mix", [P, KC])
    small("g_x", [P, KC])
    small("g_mem", [P, KC])
    small("g_moe", [P, KC])
    small("g_oa", [P, D_A // P])
    small("g_ob", [P, MB])
    small("bglu", [P, MB])
    small("dskip", [P, G])
    small("ss", [P, 32])
    small("rs", [P, 32])
    small("ones", [P, P])
    small("neg", [P, 8])
    small("half", [P, 1])
    small("warm", [P, 1])
    small("negx", [P, 8])
    small("denx", [P, 8])
    small("den", [P, 8])
    small("a8", [P, 4, G])
    small("cnt_i", [1, E], I32)
    at("xrow", 64, [P, NB, D])
    at("memrow", 80, [P, N_MEM // P, D])
    at("xnT", 96, [P, KC, S])
    for i in range(2):
        at(f"wa{i}", 128 + 16 * i, [P, KC, 512])
    at("memT", 160, [P, KC, N_MEM])
    at("junk", 160, [P, D])
    at("bn", 164, [P, 6, P])
    at("Cp", 169, [P, G, (T + 1) * CH])
    at("CrCi", 187, [P, 2, G * CH])
    at("Bri", 191, [P, 2, G, CH])
    at("lam", 195, [G, 16, ST])
    at("bb", 195, [P, 2, G, CH])
    at("tmp", 199, [P, 2, G * CH])
    at("Cn", 203, [P, 4, 2, P])
    at("BT", 64, [P, G, P])
    at("Pw", 88, [P, T + 1, 2, G])
    at("F12", 90.5, [P, 2, T + 1, G])
    at("G12", 93, [P, 2, T, G])
    at("prm", 95.25, [P, 4, G])
    at("Bm", 80, [P, G, 192])
    at("M1", 104, [P, G, P])
    at("Krow", 120, [CH, G, P])
    at("V", 120, [P, J + 1, 2, G])
    at("U", 187, [P, G, J])
    at("Y1", 64, [P, G, J])
    at("ztile", 136, [CH, G, 112])
    at("bias", 80, [P, H_A, S])
    at("sc", 152.5, [P, 2, S])
    at("pr", 112, [P, 2, S])
    at("prT", 160.5, [P, 4, 512])
    at("ya", 187, [P, NB, D_A])
    at("scan_t", 203, [P, 2, 2, G])
    at("ohb", 152.5, [ONEHOT_ROWS, LINE])
    at("rb", 157.5, [ONEHOT_ROWS, H_A])
    at("line", 158, [H_A, LINE])
    for i in range(3):
        at(f"wd{i}", 16 * i, [P, KC, 512])
    at("h", 80, [P, NB, D])
    at("yaT", 120, [P, D_A // P, S])
    at("yg", 152.5, [P, G, J])
    at("yT", 136, [P, MB, T, J])
    at("ybT", 152.5, [P, MB, S])
    at("gate_s", 187, [P, MB, S])
    at("sq", 169, [P, MB, S])
    at("hT", 120, [P, KC, S])
    at("xn", 64, [P, 4, D])
    at("qxT", 152.5, [P, H_X, S])
    at("xnb", 187, [P, 4, D])
    at("px", 169, [P, 8, N_MEM])
    at("pxT", 177, [P, 2, 2, 512])
    at("oT", 187, [P, H_X, S])
    at("junkd", 203, [P, D])
    at("wr", 112, [P, KC, E])
    at("br", 113.5, [E, 1])
    at("logitT", 170, [E, S])
    at("logit", 152.5, [P, NB, E])
    at("top8", 154, [P, NB, 8])
    at("idx8", 154.5, [P, NB, 8], U32)
    at("idxf", 155, [P, NB, 8])
    at("gates", 155.5, [P, NB, 8])
    at("gsum", 156, [P, 2, NB])
    at("m4", 156.25, [P, NB, TOPK, E])
    at("maskE", 160.5, [P, NB, E])
    at("rank", 161.5, [P, NB, E])
    at("pref", 162.5, [P, NB + 1, E])
    at("tri", 164, [P, P])
    at("iota_e", 164.5, [P, E])
    at("iota_w", 165, [P, WIN])
    at("dest", 166, [P, 4, NB * TOPK])
    at("desti", 166.75, [P, 2, NB * TOPK], I32)
    at("tok1", 167.25, [P, NB])
    at("dumpid", 167.5, [P, WIN])
    at("lo", 187, [P, 4, P])
    at("hi", 189, [P, 4, 2, WIN])
    places = [8 * i if i < 6 else 64 + 8 * (i - 6) for i in range(SLOTS)]
    m["we"] = [at(f"we{i}", kib, [P, KC, WIN]) for i, kib in enumerate(places)]
    at("xg0", 48, [P, D])
    at("xg1", 52, [P, D])
    at("xT", 112, [P, KC, WIN])
    at("act", 120, [P, KC, WIN])
    at("sg", 160, [P, 2, 2, WIN])
    at("gx", 170, [P, 2], I32)
    at("sx", 170.25, [P, 2], I32)
    at("list_f", 174, [P, 2, WIN])
    at("idx_g", 171, [P, WIN], I32)
    at("idx_s", 172, [P, WIN], I32)
    at("gate_l", 173, [P, WIN])
    at("list_t", 176, [P, 2, WIN])
    at("outT", 182, [P, KC, WIN])
    at("orow0", 190, [P, D])
    at("orow1", 194, [P, D])
    at("glu", 198, [P, 2, 2, WIN])
    at("lin", 202, [P, 2, 2, WIN])
    at("fin", 0, [P, NB, D])
    at("fout", 80, [P, NB, D])
    at("gfin", 112, [P, D])
    at("jf", 116, [P, D])
    m["ps"] = ctx.enter_context(nc.psum_tensor("ps", [P, 8, 512], F32))
    m["w_in"] = [nc.alloc_semaphore(name=f"we_in{s}") for s in range(SLOTS)]
    return namedtuple("Memory", m)(**m)


def chunked(w, cols):
    return w[:, cols].rearrange("(k p) n -> p k n", p=P)


def root(nc, m, ch, col, width, n=1):
    cols = slice(col, col + n)
    ch.link(nc.gpsimd.tensor_scalar(m.ss[:, cols], m.ss[:, cols], width * EPS, None, ALU.add))
    ch.link(nc.gpsimd.tensor_tensor(m.rs[:, cols], m.ss[:, cols], m.half[:, 0:1].to_broadcast([P, n]), ALU.pow))
    return nc.gpsimd.tensor_scalar(m.rs[:, cols], m.rs[:, cols], math.sqrt(width), None, ALU.mult)


def phase_a(nc, block, m, a, sem):
    x_in = [sem(f"x_in{b}") for b in range(NB)]
    mem_in, par_in, c_in, b_in, gain_in, mix_in, bn_in = (sem(n) for n in ("mem_in", "par_in", "c_in", "b_in", "gain_in", "mix_in", "bn_in"))
    w_in = [sem(f"wa_in{i}") for i in range(6)]
    ident_ok, squared, rooted, scaled, transposed = (sem(n) for n in ("ident_ok", "squared", "rooted", "scaled", "transposed"))
    tr_act, tr_dve, pj_act, pj_dve, grouped = (sem(n) for n in ("tr_act", "tr_dve", "pj_act", "pj_dve", "grouped"))
    u_out, lam_ok, lam_act, s5_step, act_step, prep_ok = (sem(n) for n in ("u_out", "lam_ok", "lam_act", "s5_step", "act_step", "prep_ok"))
    lam_inv = sem("lam_inv")
    units = [(a.w_in, slice(3 * D_A, 4 * D_A)), (a.w_in, slice(D_A, 2 * D_A)), (a.w_in, slice(2 * D_A, 3 * D_A)),
             (a.w_in, slice(0, D_A)), (a.w_xkv, slice(0, 512)), (a.w_xkv, slice(512, 1024))]
    PRM, CRE, B1G, B2G, MEMG = 16, 17, 19, 20, 21

    @block.sync
    def _(sp):
        sp.dma_start(m.xrow[:, 0], a.x[0:P]).then_inc(x_in[0], 16)
        for b in range(1, NB):
            sp.dma_start(m.xrow[:, b], a.x[b * P:(b + 1) * P]).then_inc(x_in[b], 16)
            if b == 3:
                sp.dma_start(m.g_mix[:], a.norm_mix.rearrange("(k p) -> p k", p=P)).then_inc(mix_in, 16)
                sp.dma_start(m.lam[:, 0, :], a.s5_a_re).then_inc(par_in, 16)
                sp.dma_start(m.lam[:, 1, :], a.s5_a_im).then_inc(par_in, 16)
                sp.dma_start(m.lam[:, 2, 0:1], a.s5_log_dt.rearrange("(g a) -> g a", a=1)).then_inc(par_in, 16)
        sp.dma_start(m.wa0[:], chunked(*units[0])).then_inc(w_in[0], 16)
        sp.dma_start(m.wa1[:], chunked(*units[1])).then_inc(w_in[1], 16)
        for dst, src in ((m.g_x, a.norm_xattn), (m.g_mem, a.norm_mem), (m.g_moe, a.norm_moe),
                         (m.g_oa, a.g_out_attn), (m.g_ob, a.g_out_ssm), (m.bglu, a.b_glu)):
            sp.dma_start(dst[:], src.rearrange("(k p) -> p k", p=P)).then_inc(gain_in, 16)
        for r, src in enumerate((a.s5_c_re, a.s5_c_im)):
            for dup in range(2):
                sp.dma_start(m.Cn[:, :, r, dup * ST:(dup + 1) * ST],
                              src.rearrange("g c p -> (g c) p").rearrange("(i q) p -> q i p", i=4)).then_inc(c_in, 16)
        for r, src in enumerate((a.s5_b_re, a.s5_b_im)):
            for dup in range(2):
                sp.dma_start(m.Bri[dup * ST:(dup + 1) * ST, r], src.rearrange("g p c -> p g c")).then_inc(b_in, 16)
        sp.dma_start(m.bn[:, 0:4], a.b1.rearrange("e (c f) -> (e c) f", f=P).rearrange("(i q) f -> q i f", i=4)).then_inc(bn_in, 16)
        sp.dma_start(m.bn[:, 4:6], a.b2.rearrange("e (c f) -> (e c) f", f=P).rearrange("(i q) f -> q i f", i=2)).then_inc(bn_in, 16)
        for t in range(T):
            sp.dma_start(m.dskip[t * CH:(t + 1) * CH, :], a.s5_d.rearrange("(g c) -> c g", c=CH)).then_inc(gain_in, 16)
        sp.wait_ge(transposed, 16)
        sp.dma_start(m.memrow[:], a.mem.rearrange("(b p) d -> p b d", p=P)).then_inc(mem_in, 16)
        for n in range(2, 6):
            sp.wait_ge(grouped, 8 * (n - 1))
            sp.dma_start((m.wa0 if n % 2 == 0 else m.wa1)[:], chunked(*units[n])).then_inc(w_in[n], 16)
            if n == 2:
                sp.wait_ge(pj_act, 4)
                sp.wait_ge(pj_dve, 4)
                sp.dma_start(a.u_dram.rearrange("(m p) n -> p m n", p=P), m.uT[:]).then_inc(u_out, 16)
        sp.wait_ge(u_out, 16)

    def tr_evac(j, out_scale):
        bank = m.ps[:, j % 4, :]
        if j < 16:
            half, k = divmod(j, 8)
            return m.xnT[:, k, half * 512:(half + 1) * 512], bank, m.g_mix[:, k:k + 1]
        if j == PRM:
            return m.prm[:, :, :], m.ps[:, j % 4, 0:P].rearrange("p (q g) -> p q g", g=G), None
        if j in (CRE, CRE + 1):
            return m.CrCi[:, j - CRE, :], bank, None
        if j == B1G:
            return m.b1T[:, :], bank, None
        if j == B2G:
            return m.b2T[:, :], m.ps[:, j % 4, 0:256], None
        k = j - MEMG
        return m.memT[:, k, :], m.ps[:, j % 4, 0:N_MEM], m.g_mem[:, k:k + 1]

    def proj_dst(i):
        bank = m.ps[:, 4 + i % 4, :]
        if i < 8:
            c, half = divmod(i, 2)
            dst = m.uT[:, c, :].rearrange("p (s j) -> p j s", s=T)[:, half * (J // 2):(half + 1) * (J // 2), :]
            return dst, bank.rearrange("p (j s) -> p j s", s=T), 1.0
        if i < 16:
            c, half = divmod(i - 8, 2)
            return m.kT[:, c, half * 512:(half + 1) * 512], bank, 1.0
        if i < 24:
            return m.v[:, i - 16, :], bank, 1.0
        if i < 32:
            c, half = divmod(i - 24, 2)
            return m.qT[:, c, half * 512:(half + 1) * 512], bank, HD_A ** -0.5
        if i < 36:
            return m.kmT[:, i - 32, :], m.ps[:, 4 + i % 4, 0:N_MEM], 1.0
        return m.vm[:, i - 36, :], bank, 1.0

    @block.scalar
    def _(act):
        for b in range(NB):
            act.wait_ge(x_in[b], 16)
            if b:
                act.wait_ge(squared, b)
            nc.scalar.activation(m.junk[:], m.xrow[:, b], ACT.Square, accum_out=m.ss[:, b:b + 1]).then_inc(squared, 1)

        def evac_tr(j):
            act.wait_ge(transposed, j + 1)
            dst, src, g = tr_evac(j, None)
            nc.scalar.activation(dst, src, ACT.Copy if g is None else ACT.Identity, **({} if g is None else {"scale": g})).then_inc(tr_act, 1)

        def evac_pj(i):
            act.wait_ge(grouped, i + 1)
            if i == 24:
                act.wait_ge(u_out, 16)
            dst, src, s = proj_dst(i)
            nc.scalar.activation(dst, src, ACT.Copy, scale=s).then_inc(pj_act, 1)

        act.wait_ge(mix_in, 16)
        for j in range(0, 16, 2):
            evac_tr(j)
            if j == 2:
                act.wait_ge(par_in, 48)
                nc.scalar.activation(m.lam[:, 2, 1:2], m.lam[:, 2, 0:1], ACT.Exp).then_inc(lam_act, 1)
            if j == 8:
                act.wait_ge(lam_ok, 1)
                nc.scalar.activation(m.lam[:, 5, :], m.lam[:, 3, :], ACT.Exp).then_inc(lam_act, 1)
        act.wait_ge(lam_ok, 2)
        nc.scalar.activation(m.lam[:, 8, :], m.lam[:, 6, :], ACT.Sin).then_inc(lam_act, 1)
        nc.scalar.activation(m.lam[:, 9, :], m.lam[:, 7, :], ACT.Sin).then_inc(lam_act, 1)
        for i in range(0, 4, 2):
            evac_pj(i)
        for j in (16, 18, 20):
            evac_tr(j)
        for i in range(4, 32, 2):
            evac_pj(i)
        act.wait_ge(gain_in, 16 * 14)
        for b in range(N_MEM // P):
            act.wait_ge(mem_in, 16)
            act.wait_ge(squared, NB + b)
            nc.scalar.activation(m.junk[:], m.memrow[:, b], ACT.Square, accum_out=m.ss[:, NB + b:NB + b + 1]).then_inc(squared, 1)
        for j in range(22, 29, 2):
            evac_tr(j)
        for i in range(32, 38, 2):
            evac_pj(i)

    @block.vector
    def _(dve):
        def norm(b, row):
            dve.wait_ge(rooted, b + 1)
            nc.vector.tensor_scalar(row, row, m.rs[:, b:b + 1], None, ALU.mult).then_inc(scaled, 1)

        def evac_tr(j):
            dve.wait_ge(transposed, j + 1)
            dst, src, g = tr_evac(j, None)
            if g is None:
                nc.vector.tensor_copy(dst, src).then_inc(tr_dve, 1)
            else:
                nc.vector.tensor_scalar(dst, src, g, None, ALU.mult).then_inc(tr_dve, 1)

        def evac_pj(i):
            dve.wait_ge(grouped, i + 1)
            if i == 25:
                dve.wait_ge(u_out, 16)
            dst, src, s = proj_dst(i)
            nc.vector.tensor_scalar(dst, src, s, None, ALU.mult).then_inc(pj_dve, 1)

        for b in range(4):
            norm(b, m.xrow[:, b])
        dve.wait_ge(mix_in, 16)
        for j in (1, 3, 5, 7):
            evac_tr(j)
            norm(4 + j // 2, m.xrow[:, 4 + j // 2])
        for j in range(9, 16, 2):
            evac_tr(j)
        dve.wait_ge(lam_ok, 3)
        nc.vector.reciprocal(m.lam[:, 6, :], m.lam[:, 6, :]).then_inc(lam_inv, 1)
        for i in range(1, 4, 2):
            evac_pj(i)
        for j in (17, 19):
            evac_tr(j)
        for i in range(5, 32, 2):
            evac_pj(i)
        dve.wait_ge(gain_in, 16 * 14)
        for b in range(N_MEM // P):
            norm(NB + b, m.memrow[:, b])
        for j in range(21, 29, 2):
            evac_tr(j)
        for i in range(33, 38, 2):
            evac_pj(i)

    @block.tensor
    def _(pe):
        pe.wait_ge(ident_ok, 2)

        def free_bank(j):
            if j >= 4:
                pe.wait_ge(tr_act if j % 2 == 0 else tr_dve, (j - 4) // 2 + 1)

        def put(j, sources, width=P):
            free_bank(j)
            for i, src in enumerate(sources):
                rows = src.shape[0]
                last = nc.tensor.transpose(m.ps[:, j % 4, i * width:i * width + rows], src, m.ident[0:rows, 0:rows])
            last.then_inc(transposed, 1)

        for half in range(2):
            pe.wait_ge(scaled, 4 * (half + 1))
            for k in range(KC):
                put(8 * half + k, [m.xrow[:, 4 * half + i, k * P:(k + 1) * P] for i in range(4)])
        group = [0]

        def project(weights, moving, width):
            i = group[0]
            if i >= 4:
                pe.wait_ge(pj_act if i % 2 == 0 else pj_dve, (i - 4) // 2 + 1)
            for k in range(KC):
                last = nc.tensor.matmul(m.ps[:, 4 + i % 4, 0:width], weights(k), moving(k), start=(k == 0), stop=(k == KC - 1))
            group[0] += 1
            return last.then_inc(grouped, 1)

        def parameters():
            pe.wait_ge(prep_ok, 1)
            put(PRM, [m.lam[:, 8 + 2 * q:10 + 2 * q, :].rearrange("g a p -> g (a p)") for q in range(4)], width=G)
            pe.wait_ge(c_in, 64)
            for r in range(2):
                put(CRE + r, [m.Cn[:, i, r, :] for i in range(4)])
            pe.wait_ge(bn_in, 32)
            put(B1G, [m.bn[:, i] for i in range(4)])
            put(B2G, [m.bn[:, 4 + i] for i in range(2)])

        pe.wait_ge(tr_act, 8)
        pe.wait_ge(tr_dve, 8)
        for n in range(4):
            w = m.wa0 if n % 2 == 0 else m.wa1
            pe.wait_ge(w_in[n], 16)
            if n == 2:
                for b in range(NB):
                    project(lambda k: m.xnT[:, k, b * P:(b + 1) * P], lambda k: w[:, k, :], 512)
            else:
                for c in range(4):
                    if n == 0 and c == 2:
                        parameters()
                    for half in range(2):
                        project(lambda k: w[:, k, c * P:(c + 1) * P],
                                       lambda k: m.xnT[:, k, half * 512:(half + 1) * 512], 512)
        pe.wait_ge(scaled, NB + 2)
        for k in range(KC):
            put(MEMG + k, [m.memrow[:, b, k * P:(k + 1) * P] for b in range(2)])
        pe.wait_ge(tr_act, 15)
        pe.wait_ge(tr_dve, 14)
        pe.wait_ge(w_in[4], 16)
        for c in range(H_X):
            project(lambda k: m.wa0[:, k, c * P:(c + 1) * P], lambda k: m.memT[:, k, :], N_MEM)
        pe.wait_ge(w_in[5], 16)
        for b in range(2):
            project(lambda k: m.memT[:, k, b * P:(b + 1) * P], lambda k: m.wa1[:, k, :], 512)

    @block.gpsimd
    def _(pool):
        nc.gpsimd.memset(m.ident[:], 0.0).then_inc(ident_ok, 1)
        pool.wait_ge(ident_ok, 1)
        nc.gpsimd.affine_select(out=m.ident[:], in_=m.ident[:], compare_op=ALU.not_equal, fill=1.0, base=0,
                                pattern=[[-1, P]], channel_multiplier=1).then_inc(ident_ok, 1)
        nc.gpsimd.memset(m.ones[:], 1.0)
        ch = Chain(pool, s5_step)
        ch.link(nc.gpsimd.memset(m.half[:], -0.5))
        for b in range(NB):
            pool.wait_ge(squared, b + 1)
            root(nc, m, ch, b, D).then_inc(rooted, 1)
        lam = m.lam
        tt, ts = nc.gpsimd.tensor_tensor, nc.gpsimd.tensor_scalar
        pool.wait_ge(lam_act, 1)
        dt = lam[:, 2, 1:2]
        ch.link(ts(lam[:, 3, :], lam[:, 0, :], dt, None, ALU.mult))
        ch.link(ts(lam[:, 4, :], lam[:, 1, :], dt, None, ALU.mult))
        pool.sem_inc(lam_ok, 1)
        MAGIC = 1.5 * 2.0 ** 23
        c1 = 6.28125
        c2 = 2028 / 2.0 ** 20
        c3 = 2 * math.pi - c1 - c2
        ch.link(ts(lam[:, 10, :], lam[:, 4, :], 1.0 / (2 * math.pi), None, ALU.mult))
        ch.link(ts(lam[:, 10, :], lam[:, 10, :], MAGIC, None, ALU.add))
        ch.link(ts(lam[:, 10, :], lam[:, 10, :], MAGIC, None, ALU.subtract))
        src = lam[:, 4, :]
        for c in (c1, c2, c3):
            ch.link(ts(lam[:, 11, :], lam[:, 10, :], c, None, ALU.mult))
            ch.link(tt(lam[:, 6, :], src, lam[:, 11, :], ALU.subtract))
            src = lam[:, 6, :]
        top = 3.1415925
        ch.link(ts(lam[:, 6, :], lam[:, 6, :], top, -top, ALU.min, ALU.max))
        ch.link(ts(lam[:, 11, :], lam[:, 6, :], math.pi / 2, -2 * math.pi, ALU.is_gt, ALU.mult))
        ch.link(ts(lam[:, 7, :], lam[:, 6, :], math.pi / 2, None, ALU.add))
        ch.link(tt(lam[:, 7, :], lam[:, 7, :], lam[:, 11, :], ALU.add))
        ch.link(ts(lam[:, 7, :], lam[:, 7, :], top, -top, ALU.min, ALU.max))
        pool.sem_inc(lam_ok, 1)
        pool.wait_ge(lam_act, 4)
        ch.link(tt(lam[:, 14, :], lam[:, 5, :], lam[:, 9, :], ALU.mult))
        ch.link(tt(lam[:, 15, :], lam[:, 5, :], lam[:, 8, :], ALU.mult))
        ch.link(ts(lam[:, 3, :], lam[:, 14, :], -1.0, None, ALU.add))
        ch.link(tt(lam[:, 6, :], lam[:, 0, :], lam[:, 0, :], ALU.mult))
        ch.link(tt(lam[:, 7, :], lam[:, 1, :], lam[:, 1, :], ALU.mult))
        ch.link(tt(lam[:, 6, :], lam[:, 6, :], lam[:, 7, :], ALU.add))
        pool.sem_inc(lam_ok, 1)
        ch.link(tt(lam[:, 7, :], lam[:, 3, :], lam[:, 0, :], ALU.mult))
        ch.link(tt(lam[:, 8, :], lam[:, 15, :], lam[:, 1, :], ALU.mult))
        ch.link(tt(lam[:, 7, :], lam[:, 7, :], lam[:, 8, :], ALU.add))
        pool.wait_ge(lam_inv, 1)
        ch.link(tt(lam[:, 12, :], lam[:, 7, :], lam[:, 6, :], ALU.mult))
        ch.link(tt(lam[:, 7, :], lam[:, 15, :], lam[:, 0, :], ALU.mult))
        ch.link(tt(lam[:, 8, :], lam[:, 3, :], lam[:, 1, :], ALU.mult))
        ch.link(tt(lam[:, 7, :], lam[:, 7, :], lam[:, 8, :], ALU.subtract))
        ch.link(tt(lam[:, 5, :], lam[:, 7, :], lam[:, 6, :], ALU.mult))
        for dst, s in ((8, 14), (9, 14), (10, 15), (11, 15), (13, 12)):
            ch.link(nc.gpsimd.tensor_copy(lam[:, dst, :], lam[:, s, :]))
        for dst, s in ((14, 5), (15, 5)):
            ch.link(nc.gpsimd.tensor_copy(lam[:, dst, :], lam[:, s, :]))
        pool.sem_inc(prep_ok, 1)
        pool.wait_ge(tr_act, PRM // 2 + 1)
        Pw, F12, G12 = m.Pw, m.F12, m.G12
        ar, ai, zr, zi = (m.prm[:, q, :] for q in range(4))
        ch.link(nc.gpsimd.memset(Pw[:, 0, 0, :], 1.0))
        ch.link(nc.gpsimd.memset(Pw[:, 0, 1, :], 0.0))
        ch.link(nc.gpsimd.tensor_copy(Pw[:, 1, :, :], m.prm[:, 0:2, :]))
        t0, t1 = m.tmp[:, 0, 0:G], m.tmp[:, 1, 0:G]
        for n in range(1, T):
            re, im = Pw[:, n, 0, :], Pw[:, n, 1, :]
            ch.link(tt(t0, re, ar, ALU.mult))
            ch.link(tt(t1, im, ai, ALU.mult))
            ch.link(tt(Pw[:, n + 1, 0, :], t0, t1, ALU.subtract))
            ch.link(tt(t0, re, ai, ALU.mult))
            ch.link(tt(t1, im, ar, ALU.mult))
            ch.link(tt(Pw[:, n + 1, 1, :], t0, t1, ALU.add))
        up, dn = slice(0, ST), slice(ST, P)
        for dst, half, part, sign in ((F12[up, 0], up, 0, 1.0), (F12[dn, 0], dn, 1, -1.0), (F12[up, 1], up, 1, -1.0),
                                      (F12[dn, 1], dn, 0, -1.0)):
            ch.link(ts(dst, Pw[half, :, part, :], sign, None, ALU.mult))
        for dst, half, part, sign in ((G12[up, 0], up, 0, 1.0), (G12[dn, 0], dn, 1, 1.0), (G12[up, 1], up, 1, -1.0),
                                      (G12[dn, 1], dn, 0, 1.0)):
            ch.link(ts(dst, Pw[half, 0:T, part, :], sign, None, ALU.mult))
        for part in range(2):
            ch.link(nc.gpsimd.tensor_copy(m.a8[:, part, :], Pw[:, T, 0, :]))
        for dst, half, sign in ((m.a8[up, 2], up, 1.0), (m.a8[dn, 2], dn, -1.0), (m.a8[up, 3], up, -1.0), (m.a8[dn, 3], dn, 1.0)):
            ch.link(ts(dst, Pw[half, T, 1, :], sign, None, ALU.mult))
        wide = [P, G, CH]

        def over(v):
            return v.unsqueeze(2).to_broadcast(wide)

        s0, s1 = (m.tmp[:, i, :].rearrange("p (g c) -> p g c", c=CH) for i in range(2))
        pool.wait_ge(b_in, 64)
        Br, Bi = m.Bri[:, 0], m.Bri[:, 1]
        ch.link(tt(s0, Br, over(zr), ALU.mult))
        ch.link(tt(s1, Bi, over(zi), ALU.mult))
        ch.link(tt(m.bb[:, 0], s0, s1, ALU.subtract))
        ch.link(tt(s0, Br, over(zi), ALU.mult))
        ch.link(tt(s1, Bi, over(zr), ALU.mult))
        ch.link(tt(m.bb[:, 1], s0, s1, ALU.add))
        pool.wait_ge(transposed, 16)
        for s in range(T):
            ch.link(tt(s0, m.bb[:, 0], over(G12[:, 0, T - 1 - s, :]), ALU.mult))
            ch.link(tt(s1, m.bb[:, 1], over(G12[:, 1, T - 1 - s, :]), ALU.mult))
            ch.link(tt(m.BT[:, :, s * CH:(s + 1) * CH], s0, s1, ALU.add))
        pool.wait_ge(tr_dve, (CRE + 1) // 2)
        pool.wait_ge(tr_act, (CRE + 1) // 2 + 1)
        Cr, Ci = (m.CrCi[:, r, :].rearrange("p (g c) -> p g c", c=CH) for r in range(2))
        for t in range(T + 1):
            ch.link(tt(s0, Cr, over(F12[:, 0, t, :]), ALU.mult))
            ch.link(tt(s1, Ci, over(F12[:, 1, t, :]), ALU.mult))
            ch.link(tt(m.Cp[:, :, t * CH:(t + 1) * CH], s0, s1, ALU.add))
        for b in range(NB, NB + N_MEM // P):
            pool.wait_ge(squared, b + 1)
            root(nc, m, ch, b, D).then_inc(rooted, 1)


def phase_b(nc, block, m, a, sem):
    U_in, zero_ok, pad_out, k_out, m1_in, bst = (sem(n) for n in ("U_in", "zero_ok", "pad_out", "k_out", "m1_in", "bst"))
    oh_in, line_mm, line_ok, line_out, skewed = (sem(n) for n in ("oh_in", "line_mm", "line_ok", "line_out", "skewed"))
    b_act, b_dve, ones_row = sem("b_act"), sem("b_dve"), sem("ones_row")
    K0, B0, V0, Y0, END = 0, 8, 16, 32, 40
    evac_by = ["dve" if i % 2 or i >= Y0 else "act" for i in range(END)]

    def copied(eng, i):
        eng.wait_ge(b_dve if evac_by[i] == "dve" else b_act, evac_by[:i + 1].count(evac_by[i]))

    @block.sync
    def _(sp):
        def skew(h):
            sp.dma_start(bass.AP(a.skew_dram.tensor, h * P * (LINE + 1), [[LINE + 1, P], [1, LINE]]),
                         a.line_dram[h:h + 1, :].to_broadcast([P, LINE])).then_inc(skewed, 16)

        for s in range(T):
            sp.dma_start(m.U[s * CH:(s + 1) * CH], a.u_dram[:, s * J:(s + 1) * J].rearrange("(g c) j -> c g j", c=CH)).then_inc(U_in, 16)
        sp.wait_ge(line_ok, 3)
        sp.dma_start(a.line_dram, m.line[:]).then_inc(line_out, 16)
        sp.wait_ge(zero_ok, 1)
        sp.dma_start(a.kp_dram[:, :, 0:112], m.ztile[:]).then_inc(pad_out, 16)
        copied(sp, B0 - 2)
        copied(sp, B0 - 1)
        sp.dma_start(a.kp_dram[:, :, 112:240], m.Krow[:]).then_inc(k_out, 16)
        sp.wait_ge(line_out, 16)
        for h in range(H_A // 2):
            skew(h)
        sp.wait_ge(pad_out, 16)
        sp.wait_ge(k_out, 16)
        for s in range(T):
            sp.dma_start(m.M1[s * CH:(s + 1) * CH], a.kp_dram[:, :, 112 - CH * s:240 - CH * s]).then_inc(m1_in, 16)
        for h in range(H_A // 2, H_A):
            skew(h)
        sp.wait_ge(skewed, 16 * H_A)

    def evac(eng, engine, i):
        eng.wait_ge(bst, i + 1)
        bank = m.ps[:, i % 6, :].rearrange("p (g n) -> p g n", g=4)
        done = b_act if evac_by[i] == "act" else b_dve
        copy = (lambda dst, src: nc.scalar.activation(dst, src, ACT.Copy)) if evac_by[i] == "act" else nc.vector.tensor_copy
        if i < B0:
            copy(m.Krow[:, 4 * i:4 * i + 4, :], bank[0:CH]).then_inc(done, 1)
        elif i < V0:
            g = 4 * (i - B0)
            copy(m.Bm[:, g:g + 4, 0:P], bank)
            copy(m.Bm[:, g:g + 4, P:P + ST], bank[:, :, 0:ST]).then_inc(done, 1)
        elif i < Y0:
            if i < V0 + 2:
                eng.wait_ge(k_out, 16)
                eng.wait_ge(pad_out, 16)
            r, q = divmod(i - V0, 8)
            copy(m.V[:, 1:J + 1, r, 4 * q:4 * q + 4], bank.rearrange("p g j -> p j g")).then_inc(done, 1)
        else:
            if i == Y0:
                eng.wait_ge(b_act, evac_by.count("act"))
            for n in range(4):
                g = 4 * (i - Y0) + n
                last = nc.vector.scalar_tensor_tensor(out=m.Y1[:, g, :], in0=m.U[:, g, :], scalar=m.dskip[:, g:g + 1],
                                                      in1=bank[:, n, :], op0=ALU.mult, op1=ALU.add)
            last.then_inc(done, 1)

    @block.scalar
    def _(act):
        act.dma_start(m.ohb[:], a.onehot).then_inc(oh_in, 16)
        act.dma_start(m.rb[0:NUM_BUCKETS], a.rel_bias).then_inc(oh_in, 16)
        for i in range(END):
            if evac_by[i] == "act":
                evac(act, nc.scalar, i)

    @block.vector
    def _(dve):
        for n in range(3):
            dve.wait_ge(line_mm, n + 1)
            nc.vector.tensor_copy(m.line[:, n * 384:(n + 1) * 384], m.ps[0:H_A, 6 + n % 2, 0:384]).then_inc(line_ok, 1)
        dve.wait_ge(U_in, 16 * T)
        for i in range(END):
            if evac_by[i] == "dve":
                evac(dve, nc.vector, i)

    @block.tensor
    def _(pe):
        def group(i, emit):
            if i >= 6:
                copied(pe, i - 6)
            for n in range(4):
                last = emit(n, m.ps[:, i % 6, n * P:(n + 1) * P])
            last.then_inc(bst, 1)

        pe.wait_ge(oh_in, 32)
        pe.wait_ge(ones_row, 1)
        for n in range(3):
            if n == 2:
                pe.wait_ge(line_ok, 1)
            nc.tensor.matmul(m.ps[0:H_A, 6 + n % 2, 0:384], m.rb[:], m.ohb[:, n * 384:(n + 1) * 384],
                             start=True, stop=True).then_inc(line_mm, 1)
        for q in range(8):
            group(K0 + q, lambda n, out: nc.tensor.matmul(out[0:CH], m.BT[:, 4 * q + n, P - CH:P], m.Cp[:, 4 * q + n, 0:P],
                                                          start=True, stop=True))
        for q in range(8):
            group(B0 + q, lambda n, out: nc.tensor.transpose(out, m.BT[:, 4 * q + n, :], m.ident[:]))
        pe.wait_ge(U_in, 16 * T)
        copied(pe, V0 - 1)
        copied(pe, V0 - 2)
        for r in range(2):
            for q in range(8):
                group(V0 + 8 * r + q, lambda n, out: nc.tensor.matmul(out, m.Bm[:, 4 * q + n, ST * r:ST * r + P],
                                                                      m.U[:, 4 * q + n, :], start=True, stop=True))
        pe.wait_ge(m1_in, 16 * T)
        for q in range(8):
            group(Y0 + q, lambda n, out: nc.tensor.matmul(out, m.M1[:, 4 * q + n, :], m.U[:, 4 * q + n, :], start=True, stop=True))

    @block.gpsimd
    def _(pool):
        nc.gpsimd.memset(m.rb[NUM_BUCKETS:ONEHOT_ROWS], 1.0).then_inc(ones_row, 1)
        nc.gpsimd.memset(m.ztile[:], 0.0).then_inc(zero_ok, 1)
        pool.wait_ge(k_out, 16)
        nc.gpsimd.memset(m.V[:, 0], 0.0).then_inc(zero_ok, 1)


def phase_c(nc, block, m, a, sem):
    bias_in = [sem(f"bias_in{h}") for h in range(H_A)]
    scored, maxed, exped, probs_t, probs_copied, valued, normed, c_step, scan_step = (
        sem(n) for n in ("scored", "maxed", "exped", "probs_t", "probs_copied", "valued", "normed", "c_step", "scan_step"))
    tiles = [(h, q) for h in range(H_A) for pair in range(NB // 2) for q in (NB - 1 - pair, pair)]
    N = len(tiles)
    halves = [-(-(q + 1) // 4) for _, q in tiles]
    before = [sum(halves[:i]) for i in range(N + 1)]

    @block.sync
    def _(sp):
        for h in range(H_A):
            src = bass.AP(a.skew_dram.tensor, h * P * (LINE + 1) + P - 1, [[LINE, P], [1, S]])
            sp.dma_start(m.bias[:, h, :], src).then_inc(bias_in[h], 16)

    @block.tensor
    def _(pe):
        def scores(i):
            h, q = tiles[i]
            if i >= 2:
                pe.wait_ge(maxed, i - 1)
            rows = slice(HD_A * (h % 2), HD_A * (h % 2) + HD_A)
            keys = P * (q + 1)
            for lo in range(0, keys, 512):
                n = min(512, keys - lo)
                last = nc.tensor.matmul(m.ps[:, 2 * (i % 2) + lo // 512, 0:n], m.qT[rows, h // 2, q * P:(q + 1) * P],
                                        m.kT[rows, h // 2, lo:lo + n], start=True, stop=True)
            last.then_inc(scored, 1)

        def transposes(i):
            q = tiles[i][1]
            pe.wait_ge(exped, i + 1)
            for n in range(halves[i]):
                g = before[i] + n
                if g >= 2:
                    pe.wait_ge(probs_copied, g - 1)
                for kb in range(4 * n, min(4 * n + 4, q + 1)):
                    last = nc.tensor.transpose(m.ps[:, 4 + g % 2, (kb % 4) * P:(kb % 4 + 1) * P],
                                               m.pr[:, i % 2, kb * P:(kb + 1) * P], m.ident[:])
                last.then_inc(probs_t, 1)

        def values(i):
            h, q = tiles[i]
            if i >= 2:
                pe.wait_ge(normed, i - 1)
            for n in range(halves[i]):
                pe.wait_ge(probs_copied, before[i] + n + 1)
                for kb in range(4 * n, min(4 * n + 4, q + 1)):
                    last = nc.tensor.matmul(m.ps[:, 6 + i % 2, 0:HD_A], m.prT[:, 2 * (i % 2) + n, (kb % 4) * P:(kb % 4 + 1) * P],
                                            m.v[:, kb, h * HD_A:(h + 1) * HD_A], start=(kb == 0), stop=(kb == q))
            last.then_inc(valued, 1)

        scores(0)
        scores(1)
        for i in range(N + 1):
            if i + 2 < N:
                scores(i + 2)
            if i < N:
                transposes(i)
            if i:
                values(i - 1)

    @block.vector
    def _(dve):
        ch = Chain(dve, c_step)

        def normalise(i):
            h, q = tiles[i]
            dve.wait_ge(valued, i + 1)
            den = m.den[:, i % 8:i % 8 + 1]
            ch.link(nc.vector.reciprocal(den, den))
            nc.vector.tensor_scalar(m.ya[:, q, h * HD_A:(h + 1) * HD_A], m.ps[:, 6 + i % 2, 0:HD_A], den, None,
                                    ALU.mult).then_inc(normed, 1)

        for i, (h, q) in enumerate(tiles):
            if i % NB == 0:
                dve.wait_ge(bias_in[h], 16)
            dve.wait_ge(scored, i + 1)
            if i >= 2:
                dve.wait_ge(exped, i - 1)
            keys = P * (q + 1)
            neg = m.neg[:, i % 8:i % 8 + 1]
            flat = m.ps[:, 2 * (i % 2):2 * (i % 2) + 2, :].rearrange("p b n -> p (b n)")
            nc.vector.tensor_tensor_reduce(out=m.sc[:, i % 2, 0:keys], in0=flat[:, 0:keys],
                                                   in1=m.bias[:, h, P * (NB - 1 - q):S], scale=-1.0, scalar=3.0e38,
                                                   op0=ALU.add, op1=ALU.min, accum_out=neg).then_inc(maxed, 1)
            if i >= 4:
                normalise(i - 4)
        for i in range(N - 4, N):
            normalise(i)

    @block.scalar
    def _(act):
        for i, (h, q) in enumerate(tiles):
            keys = P * (q + 1)
            act.wait_ge(maxed, i + 1)
            if i >= 2:
                act.wait_ge(probs_t, before[i - 1])
            if i >= 8:
                act.wait_ge(normed, i - 7)
            nc.scalar.activation(m.pr[:, i % 2, 0:keys], m.sc[:, i % 2, 0:keys], ACT.Exp, bias=m.neg[:, i % 8:i % 8 + 1], scale=-1.0,
                                 accum_out=m.den[:, i % 8:i % 8 + 1]).then_inc(exped, 1)
            for n in range(halves[i]):
                g = before[i] + n
                act.wait_ge(probs_t, g + 1)
                if i >= 2:
                    act.wait_ge(valued, i - 1)
                cols = P * min(4, q + 1 - 4 * n)
                nc.scalar.activation(m.prT[:, 2 * (i % 2) + n, 0:cols], m.ps[:, 4 + g % 2, 0:cols], ACT.Copy).then_inc(probs_copied, 1)

    @block.gpsimd
    def _(pool):
        t0, t1 = m.scan_t[:, 0], m.scan_t[:, 1]
        a8 = m.a8[:].rearrange("p (k r) g -> p k r g", k=2)
        tt = nc.gpsimd.tensor_tensor
        for j in range(J):
            now, nxt = m.V[:, j], m.V[:, j + 1]
            if j:
                pool.wait_ge(scan_step, 4 * j)
            tt(m.scan_t[:], now.unsqueeze(1).to_broadcast([P, 2, 2, G]), a8, ALU.mult).then_inc(scan_step, 1)
            pool.wait_ge(scan_step, 4 * j + 1)
            tt(nxt, nxt, t0, ALU.add).then_inc(scan_step, 1)
            pool.wait_ge(scan_step, 4 * j + 2)
            tt(nxt[:, 0], nxt[:, 0], t1[:, 1], ALU.add).then_inc(scan_step, 1)
            tt(nxt[:, 1], nxt[:, 1], t1[:, 0], ALU.add).then_inc(scan_step, 1)


def phase_d(nc, block, m, a, sem):
    wglu_in, wout_in, h_in, yg_out, y_in = sem("wglu_in"), [sem("wout_in0"), sem("wout_in1")], sem("h_in"), sem("yg_out"), sem("y_in")
    wxq_in, wxo_in, wout2_in = sem("wxq_in"), sem("wxo_in"), sem("wout2_in")
    filled, d_act, d_dve = sem("filled"), sem("d_act"), sem("d_dve")
    gelued, sq_a, sq_b, sq_h, rooted_d, step_pool, step_dve, step_act = (
        sem(n) for n in ("gelued", "sq_a", "sq_b", "sq_h", "rooted_d", "step_pool", "step_dve", "step_act"))
    gated, scaled_b, h_ready, xn_ready, maxed_x, exped_x, px_ready, y_added = (
        sem(n) for n in ("gated", "scaled_b", "h_ready", "xn_ready", "maxed_x", "exped_x", "px_ready", "y_added"))
    groups, at = [], {}

    def plan(name, count, by):
        at[name] = len(groups)
        groups.extend(by if isinstance(by, list) else [by] * count)

    both = ["act", "dve"]
    plan("Y", 8, "dve")
    plan("YA", 8, both * 4)
    plan("PA", 16, "dve")
    plan("GL", 8, "act")
    plan("SS", 1, "dve")
    plan("PB", 16, "dve")
    plan("HT", 16, both * 8)
    plan("XQ", 8, both * 4)
    for blk in range(2):
        plan(("S", blk), 2, "act")
    for blk in range(9):
        if blk < 8:
            plan(("T", blk), 2, both)
        if blk + 2 < 8:
            plan(("S", blk + 2), 2, "act")
        if blk:
            plan(("O", blk - 1), 1, "dve")
    plan("XO", 16, "dve")

    def bank(i):
        return m.ps[:, i % 8, :]

    def copied(eng, i):
        eng.wait_ge(d_dve if groups[i] == "dve" else d_act, groups[:i + 1].count(groups[i]))

    def scaled_copy(who, i, dst, src, g):
        if who == "act":
            nc.scalar.activation(dst, src, ACT.Identity, scale=g).then_inc(d_act, 1)
        else:
            nc.vector.tensor_scalar(dst, src, g, None, ALU.mult).then_inc(d_dve, 1)

    def spread_copy(who, eng, name, i):
        n = at[name] + i
        if groups[n] != who:
            return
        eng.wait_ge(filled, n + 1)
        half, k = divmod(i, 8)
        if name == "YA":
            half, k = divmod(i, 4)
            scaled_copy(who, n, m.yaT[:, k, half * 512:(half + 1) * 512], bank(n), m.g_oa[:, k:k + 1])
        elif name == "HT":
            scaled_copy(who, n, m.hT[:, k, half * 512:(half + 1) * 512], bank(n), m.g_x[:, k:k + 1])
        else:
            c, half = divmod(i, 2)
            scaled_copy(who, n, m.qxT[:, c, half * 512:(half + 1) * 512], bank(n), 1.0)

    blocks = [(hd, half) for hd in range(H_X) for half in range(2)]
    scale_x = HD_X ** -0.5

    @block.sync
    def _(sp):
        for n in range(2):
            sp.dma_start((m.wd1, m.wd2)[n][:, 0:4], chunked(a.w_out[0:D_A], slice(512 * n, 512 * n + 512))).then_inc(wout_in[n], 16)
        sp.dma_start(m.h[:], a.x.rearrange("(b p) d -> p b d", p=P)).then_inc(h_in, 16)
        for n in range(2):
            sp.dma_start((m.wd1, m.wd2)[n][:, 4:8], chunked(a.w_out[D_A:D], slice(512 * n, 512 * n + 512))).then_inc(wout2_in, 16)
        sp.dma_start(m.wd0[:, 0:MB], a.w_glu.rearrange("(k p) n -> p k n", p=P)).then_inc(wglu_in, 16)
        sp.wait_ge(gelued, 8)
        for t in range(T):
            sp.dma_start(a.y_dram[:, :, t, :].rearrange("g c j -> c g j"), m.yg[t * CH:(t + 1) * CH]).then_inc(yg_out, 16)
        sp.wait_ge(yg_out, 16 * T)
        sp.dma_start(m.yT[:], a.y_dram.rearrange("(m g) c t j -> (g c) m t j", m=MB)).then_inc(y_in, 16)
        sp.wait_ge(filled, at["SS"])
        sp.dma_start(m.wd0[:], chunked(a.w_xq, slice(0, 512))).then_inc(wxq_in, 16)
        sp.wait_ge(filled, at["HT"])
        sp.dma_start(m.wd1[:].rearrange("p k n -> p (k n)").rearrange("p (k n) -> p k n", k=H_X),
                     a.w_xo.rearrange("(k p) n -> p k n", p=P)).then_inc(wxo_in, 16)

    @block.tensor
    def _(pe):
        count = [0]

        def group(emit):
            i = count[0]
            if i >= 8:
                copied(pe, i - 8)
            emit(bank(i)).then_inc(filled, 1)
            count[0] += 1

        def product(weights, moving, width, kc):
            def emit(out):
                for k in range(kc):
                    last = nc.tensor.matmul(out[:, 0:width], weights(k), moving(k), start=(k == 0), stop=(k == kc - 1))
                return last
            group(emit)

        def transposes(sources):
            def emit(out):
                for n, src in enumerate(sources):
                    last = nc.tensor.transpose(out[:, n * P:(n + 1) * P], src, m.ident[:])
                return last
            group(emit)

        def emit_y(q):
            def emit(out):
                for n in range(4):
                    last = nc.tensor.matmul(out[:, n * P:(n + 1) * P], m.Cp[:, 4 * q + n, CH:CH + P], m.V[:, 0:J, 0, 4 * q + n],
                                            start=True, stop=True)
                return last
            group(emit)

        for q in range(8):
            emit_y(q)
        for half in range(2):
            for k in range(4):
                transposes([m.ya[:, 4 * half + n, k * P:(k + 1) * P] for n in range(4)])
        copied(pe, at["YA"] + 6)
        copied(pe, at["YA"] + 7)
        for n in range(2):
            pe.wait_ge(wout_in[n], 16)
        for b in range(NB):
            for n in range(2):
                product(lambda k: m.yaT[:, k, b * P:(b + 1) * P], lambda k: (m.wd1, m.wd2)[n][:, k, :], 512, 4)
        pe.wait_ge(wglu_in, 16)
        pe.wait_ge(y_in, 16)
        yflat = m.yT[:].rearrange("p m t j -> p m (t j)")
        for c in range(MB):
            for half in range(2):
                product(lambda k: m.wd0[:, k, c * P:(c + 1) * P], lambda k: yflat[:, k, half * 512:(half + 1) * 512], 512, MB)
        pe.wait_ge(sq_b, MB)

        def emit_ss(out):
            for b in range(NB):
                for c in range(MB):
                    last = nc.tensor.matmul(out[:, b:b + 1], m.sq[:, c, b * P:(b + 1) * P], m.ones[:, 0:1], start=(c == 0), stop=(c == MB - 1))
            return last
        group(emit_ss)
        pe.wait_ge(scaled_b, MB)
        pe.wait_ge(wout2_in, 32)
        for b in range(NB):
            for n in range(2):
                product(lambda k: m.ybT[:, k, b * P:(b + 1) * P], lambda k: (m.wd1, m.wd2)[n][:, 4 + k, :], 512, 4)
        for half in range(2):
            pe.wait_ge(xn_ready, 4 * (half + 1))
            for k in range(KC):
                transposes([(m.xn, m.xnb)[half][:, n, k * P:(k + 1) * P] for n in range(4)])
        copied(pe, at["HT"] + 14)
        copied(pe, at["HT"] + 15)
        pe.wait_ge(wxq_in, 16)
        for c in range(H_X):
            for half in range(2):
                product(lambda k: m.wd0[:, k, c * P:(c + 1) * P], lambda k: m.hT[:, k, half * 512:(half + 1) * 512], 512, KC)
        copied(pe, at["XQ"] + 6)
        copied(pe, at["XQ"] + 7)

        def emit_scores(blk):
            hd, half = blocks[blk]
            for pair in range(2):
                def emit(out):
                    for n in range(2):
                        q = 4 * half + 2 * pair + n
                        last = nc.tensor.matmul(out[:, n * N_MEM:(n + 1) * N_MEM], m.qxT[:, hd, q * P:(q + 1) * P], m.kmT[:, hd, :],
                                                start=True, stop=True)
                    return last
                group(emit)

        emit_scores(0)
        emit_scores(1)
        for blk in range(9):
            if blk < 8:
                pe.wait_ge(px_ready, blk + 1)
                for c in range(2):
                    transposes([m.px[:, 4 * (blk % 2) + n, c * P:(c + 1) * P] for n in range(4)])
            if blk + 2 < 8:
                emit_scores(blk + 2)
            if blk:
                hd, half = blocks[blk - 1]
                for c in range(2):
                    copied(pe, at[("T", blk - 1)] + c)
                product(lambda k: m.vm[:, k, hd * P:(hd + 1) * P], lambda k: m.pxT[:, (blk - 1) % 2, k, :], 512, 2)
        copied(pe, at[("O", 7)])
        pe.wait_ge(wxo_in, 16)
        wxo = m.wd1[:].rearrange("p k n -> p (k n)").rearrange("p (k n) -> p k n", k=H_X)
        for b in range(NB):
            for n in range(2):
                product(lambda k: m.oT[:, k, b * P:(b + 1) * P], lambda k: wxo[:, k, n * 512:(n + 1) * 512], 512, H_X)

    @block.vector
    def _(dve):
        ch = Chain(dve, step_dve)
        for q in range(8):
            n = at["Y"] + q
            dve.wait_ge(filled, n + 1)
            nc.vector.tensor_tensor(m.yg[:, 4 * q:4 * q + 4, :], bank(n).rearrange("p (g j) -> p g j", g=4),
                                    m.Y1[:, 4 * q:4 * q + 4, :], ALU.add).then_inc(d_dve, 1)
        for i in range(8):
            spread_copy("dve", dve, "YA", i)

        def add_to_h(name, i, col):
            b, n = divmod(i, 2)
            dve.wait_ge(filled, at[name] + i + 1)
            out = m.h[:, b, n * 512:(n + 1) * 512]
            if col is None:
                return nc.vector.tensor_tensor(out, out, bank(at[name] + i), ALU.add).then_inc(d_dve, 1)
            return nc.vector.scalar_tensor_tensor(out=out, in0=bank(at[name] + i), scalar=m.rs[:, col + b:col + b + 1], in1=out,
                                                  op0=ALU.mult, op1=ALU.add).then_inc(d_dve, 1)

        dve.wait_ge(h_in, 16)
        dve.wait_ge(rooted_d, 1)
        for i in range(16):
            add_to_h("PA", i, 10)
        dve.wait_ge(y_in, 16)
        for i in range(8):
            c, half = divmod(i, 2)
            copied(dve, at["GL"] + i)
            dst = m.ybT[:, c, :].rearrange("p (j t) -> p t j", t=T)[:, 4 * half:4 * half + 4, :]
            nc.vector.tensor_tensor(dst, m.yT[:, c, 4 * half:4 * half + 4, :],
                                    m.gate_s[:, c, half * 512:(half + 1) * 512].rearrange("p (t j) -> p t j", t=4),
                                    ALU.mult).then_inc(gated, 1)
        for c in range(MB):
            dve.wait_ge(sq_b, c + 1)
            nc.vector.tensor_scalar(m.ybT[:, c, :], m.ybT[:, c, :], m.g_ob[:, c:c + 1], None, ALU.mult).then_inc(scaled_b, 1)
        dve.wait_ge(filled, at["SS"] + 1)
        nc.vector.tensor_copy(m.ss[:, 18:26], bank(at["SS"])[:, 0:NB]).then_inc(d_dve, 1)
        dve.wait_ge(rooted_d, 2)
        copied(dve, at["PA"] + 15)

        def norm(b):
            dve.wait_ge(rooted_d, 3 + b)
            dst = (m.xn, m.xnb)[b // 4][:, b % 4, :]
            nc.vector.tensor_scalar(dst, m.h[:, b], m.rs[:, b:b + 1], None, ALU.mult).then_inc(xn_ready, 1)

        for b in range(NB):
            for n in range(2):
                add_to_h("PB", 2 * b + n, 18)
            if b >= 2:
                norm(b - 2)
        norm(NB - 2)
        norm(NB - 1)
        for i in range(16):
            spread_copy("dve", dve, "HT", i)
        for i in range(8):
            spread_copy("dve", dve, "XQ", i)

        def softmax_front(blk):
            cols = slice(4 * (blk % 2), 4 * (blk % 2) + 4)
            for pair in range(2):
                g = at[("S", blk)] + pair
                dve.wait_ge(filled, g + 1)
                ch.step(nc.vector.reduce_max(m.negx[:, cols][:, 2 * pair:2 * pair + 2], bank(g).rearrange("p (n k) -> p n k", n=2), AX.X))
            dve.wait_ge(ch.sem, ch.n)
            nc.vector.tensor_scalar(m.negx[:, cols], m.negx[:, cols], -scale_x, None, ALU.mult).then_inc(maxed_x, 1)

        def softmax_back(blk):
            cols = slice(4 * (blk % 2), 4 * (blk % 2) + 4)
            dve.wait_ge(exped_x, 4 * blk + 4)
            ch.link(nc.vector.reciprocal(m.denx[:, cols], m.denx[:, cols]))
            px = m.px[:, cols, :]
            nc.vector.tensor_tensor(px, px, m.denx[:, cols].unsqueeze(2).to_broadcast([P, 4, N_MEM]), ALU.mult).then_inc(px_ready, 1)

        softmax_front(0)
        softmax_front(1)
        softmax_back(0)
        for blk in range(9):
            if blk < 8:
                g = at[("T", blk)] + 1
                dve.wait_ge(filled, g + 1)
                if blk >= 2:
                    dve.wait_ge(filled, at[("O", blk - 2)] + 1)
                nc.vector.tensor_copy(m.pxT[:, blk % 2, 1, :], bank(g)).then_inc(d_dve, 1)
            if blk + 1 < 8:
                softmax_back(blk + 1)
            if blk + 2 < 8:
                softmax_front(blk + 2)
            if blk:
                hd, half = blocks[blk - 1]
                g = at[("O", blk - 1)]
                dve.wait_ge(filled, g + 1)
                nc.vector.tensor_copy(m.oT[:, hd, half * 512:(half + 1) * 512], bank(g)).then_inc(d_dve, 1)
        copied(dve, at["PB"] + 15)
        for b in range(NB):
            for n in range(2):
                add_to_h("XO", 2 * b + n, None)
            if b >= 4:
                dve.wait_ge(rooted_d, 2 + NB + b - 4 + 1)
                nc.vector.tensor_scalar(m.xn[:, b - 4, :], m.h[:, b - 4], m.rs[:, b - 4:b - 3], None, ALU.mult)

    @block.scalar
    def _(act):
        ch = Chain(act, step_act)
        for q in range(8):
            copied(act, at["Y"] + q)
            yg = m.yg[:, 4 * q:4 * q + 4, :]
            nc.scalar.activation(yg, yg, ACT.Gelu).then_inc(gelued, 1)
        for i in range(8):
            spread_copy("act", act, "YA", i)
        for b in range(NB):
            ch.link(nc.scalar.activation(m.junkd[:, 0:D_A], m.ya[:, b], ACT.Square, accum_out=m.ss[:, 10 + b:11 + b]))
        act.sem_inc(sq_a, 1)
        copied(act, at["YA"] + 7)
        for i in range(8):
            c, half = divmod(i, 2)
            act.wait_ge(filled, at["GL"] + i + 1)
            nc.scalar.activation(m.gate_s[:, c, half * 512:(half + 1) * 512], bank(at["GL"] + i), ACT.Sigmoid,
                                 bias=m.bglu[:, c:c + 1]).then_inc(d_act, 1)
        for c in range(MB):
            act.wait_ge(gated, 2 * (c + 1))
            nc.scalar.activation(m.sq[:, c, :], m.ybT[:, c, :], ACT.Square).then_inc(sq_b, 1)
        for b in range(NB):
            copied(act, at["PB"] + 2 * b + 1)
            ch.link(nc.scalar.activation(m.junkd[:], m.h[:, b], ACT.Square, accum_out=m.ss[:, b:b + 1]))
            act.sem_inc(sq_h, 1)
        for i in range(16):
            spread_copy("act", act, "HT", i)
        for i in range(8):
            spread_copy("act", act, "XQ", i)

        def exps(blk):
            act.wait_ge(maxed_x, blk + 1)
            if blk >= 2:
                act.wait_ge(filled, at[("T", blk - 2)] + 2)
            for n in range(4):
                i = 4 * blk + n
                src = bank(at[("S", blk)] + n // 2)[:, (n % 2) * N_MEM:(n % 2 + 1) * N_MEM]
                ch.link(nc.scalar.activation(m.px[:, i % 8, :], src, ACT.Exp, scale=scale_x,
                                             bias=m.negx[:, i % 8:i % 8 + 1], accum_out=m.denx[:, i % 8:i % 8 + 1]))
                act.sem_inc(exped_x, 1)
                if n % 2:
                    act.sem_inc(d_act, 1)

        exps(0)
        exps(1)
        for blk in range(8):
            g = at[("T", blk)]
            act.wait_ge(filled, g + 1)
            if blk >= 2:
                act.wait_ge(filled, at[("O", blk - 2)] + 1)
            nc.scalar.activation(m.pxT[:, blk % 2, 0, :], bank(g), ACT.Copy).then_inc(d_act, 1)
            if blk + 2 < 8:
                exps(blk + 2)
        for b in range(NB):
            copied(act, at["XO"] + 2 * b + 1)
            ch.link(nc.scalar.activation(m.junkd[:], m.h[:, b], ACT.Square, accum_out=m.ss[:, b:b + 1]))
            act.sem_inc(sq_h, 1)

    @block.gpsimd
    def _(pool):
        ch = Chain(pool, step_pool)
        pool.wait_ge(sq_a, 1)
        root(nc, m, ch, 10, D_A, NB).then_inc(rooted_d, 1)
        copied(pool, at["SS"])
        root(nc, m, ch, 18, D_B, NB).then_inc(rooted_d, 1)
        for b in range(NB):
            pool.wait_ge(sq_h, b + 1)
            root(nc, m, ch, b, D).then_inc(rooted_d, 1)
        pool.wait_ge(xn_ready, NB)
        for b in range(NB):
            pool.wait_ge(sq_h, NB + b + 1)
            root(nc, m, ch, b, D).then_inc(rooted_d, 1)


def phase_e(nc, block, m, a, sem):
    wr_in, acc_out, xn_out = sem("wr_in"), sem("acc_out"), sem("xn_out")
    xn3, step_dve = sem("xn3"), sem("step_dve_e")
    filled, e_act, e_dve = sem("filled_e"), sem("e_act"), sem("e_dve")
    consts, diffed, exped, mask_ok, onehots, gates_ok = (sem(n) for n in ("consts", "diffed", "exped_e", "mask_ok", "onehots", "gates_ok"))
    HT, LG, LT, RK, LS = 0, 16, 18, 19, 21
    PAIRS = NB * TOPK

    def copied(eng, i):
        if i < HT + 16:
            eng.wait_ge(e_act if i % 2 == 0 else e_dve, i // 2 + 1)
        else:
            eng.wait_ge(e_dve, 8 + i - LG + 1)

    def bank(i):
        return m.ps[:, i % 8, :]

    @block.sync
    def _(sp):
        sp.dma_start(a.acc_dram[0:S].rearrange("(b p) d -> p b d", p=P), m.h[:]).then_inc(acc_out, 16)
        sp.dma_start(a.acc_dram[S:S + WIN].rearrange("(b p) d -> p b d", p=P), m.h[:, 0:WIN // P]).then_inc(acc_out, 16)
        for half in range(2):
            if half:
                sp.wait_ge(xn3, 4)
            sp.dma_start(a.xn_dram[512 * half:512 * half + 512].rearrange("(b p) d -> p b d", p=P), (m.xn, m.xnb)[half][:]).then_inc(xn_out, 16)
        sp.wait_ge(acc_out, 32)
        sp.wait_ge(xn_out, 32)
        sp.wait_ge(xn3, 4)
        sp.wait_ge(filled, 16)
        for s in range(SLOTS):
            sp.dma_start(m.we[s][:], slot_source(a, s, 0)).then_inc(m.w_in[s], 16)

    @block.scalar
    def _(act):
        act.dma_start(m.wr[:], a.w_router.rearrange("(k p) n -> p k n", p=P)).then_inc(wr_in, 16)
        act.dma_start(m.br[:], a.b_router.rearrange("(n a) -> n a", a=1)).then_inc(wr_in, 16)
        for i in range(0, 16, 2):
            half, k = divmod(i, 8)
            act.wait_ge(filled, i + 1)
            nc.scalar.activation(m.hT[:, k, half * 512:(half + 1) * 512], bank(i), ACT.Identity, scale=m.g_moe[:, k:k + 1]).then_inc(e_act, 1)
        act.wait_ge(diffed, 1)
        nc.scalar.activation(m.gates[:, :, 0:TOPK], m.gates[:, :, 0:TOPK], ACT.Exp).then_inc(exped, 1)

    @block.tensor
    def _(pe):
        for half in range(2):
            if half:
                pe.wait_ge(xn3, 4)
            for k in range(KC):
                i = 8 * half + k
                if i >= 8:
                    copied(pe, i - 8)
                for n in range(4):
                    last = nc.tensor.transpose(bank(i)[:, n * P:(n + 1) * P], (m.xn, m.xnb)[half][:, n, k * P:(k + 1) * P], m.ident[:])
                last.then_inc(filled, 1)
        pe.wait_ge(e_act, 8)
        pe.wait_ge(e_dve, 8)
        pe.wait_ge(wr_in, 32)
        for half in range(2):
            for k in range(KC):
                last = nc.tensor.matmul(bank(LG + half)[0:E, :], m.wr[:, k, :], m.hT[:, k, half * 512:(half + 1) * 512],
                                        start=(k == 0), stop=(k == KC - 1))
            last.then_inc(filled, 1)
        for b in range(NB):
            if b % 4 == 0:
                copied(pe, LG + b // 4)
            last = nc.tensor.transpose(bank(LT)[:, b * E:(b + 1) * E], m.logitT[:, b * P:(b + 1) * P], m.ident[0:E, 0:E])
        last.then_inc(filled, 1)
        pe.wait_ge(mask_ok, 1)
        pe.wait_ge(consts, 4)
        mask = m.maskE[:].rearrange("p b e -> p (b e)")
        nc.tensor.matmul(bank(RK)[:, 0:NB * E], m.tri[:], mask, start=True, stop=True).then_inc(filled, 1)
        nc.tensor.matmul(bank(RK + 1)[:, 0:NB * E], m.ones[:], mask, start=True, stop=True).then_inc(filled, 1)
        for n in range(PAIRS):
            pe.wait_ge(onehots, 3 * (n + 1))
            nc.tensor.matmul(bank(LS), m.lo[:, n % 4, :], m.hi[:, n % 4].rearrange("p a w -> p (a w)"),
                             start=(n == 0), stop=(n == PAIRS - 1)).then_inc(filled, 1)

    @block.vector
    def _(dve):
        ch = Chain(dve, step_dve)
        v = nc.vector
        for b in range(4, NB):
            v.tensor_scalar(m.xnb[:, b - 4, :], m.h[:, b], m.rs[:, b:b + 1], None, ALU.mult).then_inc(xn3, 1)
        for i in range(1, 16, 2):
            half, k = divmod(i, 8)
            dve.wait_ge(filled, i + 1)
            v.tensor_scalar(m.hT[:, k, half * 512:(half + 1) * 512], bank(i), m.g_moe[:, k:k + 1], None, ALU.mult).then_inc(e_dve, 1)
        dve.wait_ge(wr_in, 32)
        for half in range(2):
            dve.wait_ge(filled, LG + half + 1)
            v.tensor_scalar(m.logitT[:, half * 512:(half + 1) * 512], bank(LG + half)[0:E, :], m.br[:], None, ALU.add).then_inc(e_dve, 1)
        dve.wait_ge(filled, LT + 1)
        v.tensor_copy(m.logit[:].rearrange("p b e -> p (b e)"), bank(LT)[:, 0:NB * E]).then_inc(e_dve, 1)
        dve.wait_ge(e_dve, 11)
        for b in range(NB):
            last = v.max(m.top8[:, b, :], m.logit[:, b, :])
            ch.step(last)
        dve.wait_ge(ch.sem, ch.n)
        for b in range(NB):
            ch.step(v.max_index(m.idx8[:, b, :], m.top8[:, b, :], m.logit[:, b, :]))
        v.tensor_tensor(m.gates[:, :, 0:TOPK], m.top8[:, :, 0:TOPK], m.top8[:, :, 0:1].to_broadcast([P, NB, TOPK]),
                        ALU.subtract).then_inc(diffed, 1)
        dve.wait_ge(ch.sem, ch.n)
        ch.link(v.tensor_copy(m.idxf[:], m.idx8[:]))
        four = [P, NB, TOPK, E]
        dve.wait_ge(consts, 4)
        for k in range(TOPK):
            ch.step(v.tensor_tensor(m.m4[:, :, k, :], m.idxf[:, :, k:k + 1].to_broadcast([P, NB, E]),
                                    m.iota_e[:].unsqueeze(1).to_broadcast([P, NB, E]), ALU.is_equal))
        dve.wait_ge(ch.sem, ch.n)
        v.reduce_sum(m.maskE[:], m.m4[:].rearrange("p b k e -> p b e k"), AX.X).then_inc(mask_ok, 1)
        dve.wait_ge(exped, 1)
        ch.link(v.reduce_sum(m.gsum[:, 0, :], m.gates[:, :, 0:TOPK], AX.X))
        ch.link(v.reciprocal(m.gsum[:, 1, :], m.gsum[:, 0, :]))
        ch.link(v.tensor_tensor(m.gates[:, :, 0:TOPK], m.gates[:, :, 0:TOPK],
                                m.gsum[:, 1, :].unsqueeze(2).to_broadcast([P, NB, TOPK]), ALU.mult))
        dve.wait_ge(filled, RK + 2)
        ch.link(v.memset(m.pref[:, 0, :], 0.0))
        for b in range(NB):
            ch.link(v.tensor_tensor(m.pref[:, b + 1, :], m.pref[:, b, :], bank(RK + 1)[:, b * E:(b + 1) * E], ALU.add))
        ch.link(v.tensor_tensor(m.rank[:].rearrange("p b e -> p (b e)"), bank(RK)[:, 0:NB * E],
                                m.pref[:, 0:NB, :].rearrange("p b e -> p (b e)"), ALU.add))
        ch.link(v.tensor_copy(m.cnt_i[:], m.pref[0:1, NB, :]))
        ch.link(v.tensor_scalar(m.cnt_i[:, 0:1], m.pref[0:1, NB, 0:1], 1.0, None, ALU.max))
        dve.sem_inc(e_dve, 2)
        for k in range(TOPK):
            ch.step(v.tensor_tensor(m.m4[:, :, k, :], m.m4[:, :, k, :], m.rank[:], ALU.mult))
        dve.wait_ge(ch.sem, ch.n)
        rk, lof, hif = m.dest[:, 0], m.dest[:, 1], m.dest[:, 2]
        ch.link(v.reduce_sum(rk.rearrange("p (b k) -> p b k", k=TOPK), m.m4[:], AX.X))
        ri, li = m.desti[:, 0], m.desti[:, 1]
        ch.link(v.tensor_copy(ri, rk))
        ch.link(v.tensor_scalar(li, ri, P - 1, None, ALU.bitwise_and))
        ch.link(v.tensor_copy(lof, li))
        ch.link(v.tensor_tensor(rk, rk, lof, ALU.subtract))
        ch.link(v.tensor_scalar(rk, rk, 1.0 / P, None, ALU.mult))
        ch.link(v.scalar_tensor_tensor(out=hif.rearrange("p (b k) -> p b k", k=TOPK), in0=m.idxf[:, :, 0:TOPK], scalar=float(S // P),
                                       in1=rk.rearrange("p (b k) -> p b k", k=TOPK), op0=ALU.mult, op1=ALU.add))
        dve.wait_ge(xn_out, 32)
        for n in range(PAIRS):
            if n >= 4:
                dve.wait_ge(filled, RK + 2 + n - 3)
            b, k = divmod(n, TOPK)
            v.tensor_scalar(m.lo[:, n % 4, :], m.iota_w[:, 0:P], lof[:, n:n + 1], None, ALU.is_equal).then_inc(onehots, 1)
            v.tensor_scalar(m.hi[:, n % 4, 0, :], m.iota_w[:], hif[:, n:n + 1], m.tok1[:, b:b + 1], ALU.is_equal, ALU.mult).then_inc(onehots, 1)
            v.tensor_scalar(m.hi[:, n % 4, 1, :], m.iota_w[:], hif[:, n:n + 1], m.gates[:, b, k:k + 1], ALU.is_equal, ALU.mult).then_inc(onehots, 1)
        dve.wait_ge(filled, LS + PAIRS)
        ch.link(v.tensor_copy(m.list_f[:].rearrange("p a w -> p (a w)"), bank(LS)))
        tok, empty = m.list_f[:, 0], m.list_t[:, 0]
        ch.link(v.tensor_copy(m.gate_l[:], m.list_f[:, 1]))
        ch.link(v.tensor_scalar(empty, tok, 0.0, None, ALU.is_equal))
        ch.link(v.scalar_tensor_tensor(out=m.list_t[:, 1], in0=empty, scalar=4096.0, in1=tok, op0=ALU.mult, op1=ALU.add))
        ch.link(v.tensor_scalar(m.idx_g[:], m.list_t[:, 1], -1.0, None, ALU.add))
        ch.link(v.tensor_tensor(empty, empty, m.dumpid[:], ALU.mult))
        ch.link(v.tensor_tensor(empty, empty, tok, ALU.add))
        ch.link(v.tensor_scalar(m.idx_s[:], empty, -1.0, None, ALU.add))

    @block.gpsimd
    def _(pool):
        g = nc.gpsimd
        for buf in (m.xg0, m.xg1):
            g.memset(buf[:], 0.0)
        g.memset(m.tri[:], 1.0).then_inc(consts, 1)
        g.iota(m.iota_e[:], [[1, E]], base=0, channel_multiplier=0, allow_small_or_imprecise_dtypes=True)
        g.iota(m.iota_w[:], [[1, WIN]], base=0, channel_multiplier=0, allow_small_or_imprecise_dtypes=True).then_inc(consts, 1)
        g.iota(m.tok1[:], [[P, NB]], base=1, channel_multiplier=1, allow_small_or_imprecise_dtypes=True)
        g.iota(m.dumpid[:], [[0, WIN // 2], [P, 2]], base=DUMP + 1, channel_multiplier=1, allow_small_or_imprecise_dtypes=True).then_inc(consts, 1)
        pool.wait_ge(consts, 1)
        g.affine_select(out=m.tri[:], in_=m.tri[:], compare_op=ALU.is_gt, fill=0.0, base=0, pattern=[[1, P]],
                        channel_multiplier=-1).then_inc(consts, 1)


def slot_source(a, s, e):
    if s < L1S:
        lo = F * (s % 2) + WIN * (s // 2)
        src = a.w1[bass.ds(e, 1), :, lo:lo + WIN]
    else:
        lo = WIN * (s - L1S)
        src = a.w2[bass.ds(e, 1), :, lo:lo + WIN]
    return src.rearrange("o (k p) n -> p (o k) n", p=P)


def each_task(eng, m, name, body):
    done, count = eng.alloc_register(f"tasks_{name}"), eng.alloc_register(f"count_{name}")
    eng.reg_mov(done, 0)

    def window(e, w, left):
        body(e, w, eng.snap(done, min_val=0, max_val=E * NWIN), left)
        eng.reg_add(done, done, 1)

    with eng.Fori(0, E) as e:
        eng.reg_load(count, m.cnt_i[0:1, bass.ds(e, 1)])
        held = eng.snap(count, min_val=0, max_val=S)
        with eng.If(held > 0):
            window(e, 0, held)
        with eng.If(held > WIN):
            with eng.Fori(1, NWIN) as w:
                left = eng.snap(held - w * WIN)
                with eng.If(left > 0):
                    window(e, w, left)
    return done


def phase_f(nc, block, m, a, sem):
    w_in = m.w_in
    gathered, scattered = [sem("gathered0"), sem("gathered1")], [sem("scattered0"), sem("scattered1")]
    x_full, xt_act, xt_dve, l1_full, glu_ok, lin_ok, swished, acted = (
        sem(n) for n in ("x_full", "xt_act", "xt_dve", "l1_full", "glu_ok", "lin_ok", "swished", "acted"))
    l2_full, biased, o_full, o_ready, step_f, init_f, idx_step = (
        sem(n) for n in ("l2_full", "biased", "o_full", "o_ready", "step_f", "init_f", "idx_step"))
    sx_step = sem("sx_step")
    psum_init, rows_in, rows_out, pool_seen, act_seen, warmed, pe_seen = (sem(n) for n in ("psum_init", "rows_in", "rows_out", "pool_seen", "act_seen", "warmed", "pe_seen"))
    JF = F // P

    OUT_BANKS = (0, 1, 7, 0)

    def parts(width):
        return 2 * (width // P)

    def by_width(eng, left, body):
        with eng.If(left < P + 1):
            body(P)
        with eng.If(left > P):
            body(WIN)

    @block.sync
    def _(sp):
        def body(e, w, n, left):
            with sp.If(n > 0):
                for s in range(SLOTS):
                    if s < L1S:
                        sp.wait_ge(l1_full, n * JF + 2 * (s // 2) + 2)
                    else:
                        sp.wait_ge(l2_full, n * KC + 2 * (s - L1S) + 2)
                    sp.dma_start(m.we[s][:], slot_source(a, s, e)).then_inc(w_in[s], 16)

        each_task(sp, m, "sp", body)

    @block.gpsimd
    def _(pool):
        g = nc.gpsimd
        g.iota(m.sx[:], [[P, 2]], base=DUMP, channel_multiplier=1).then_inc(init_f, 1)
        pool.wait_ge(init_f, 1)
        pool.sem_inc(sx_step, 2)
        left1, left2, column1, column2, gathers1, scatters1 = (
            pool.alloc_register(r) for r in ("left1", "left2", "column1", "column2", "gathers1", "scatters1"))
        for r in (left1, left2, column1, column2, gathers1, scatters1):
            pool.reg_mov(r, 0)
        xg, orow = (m.xg0, m.xg1), (m.orow0, m.orow1)
        last_row, last_token = pool.to_reg(S + WIN - 1), pool.to_reg(S - 1)

        def value(r, top):
            return pool.snap(r, min_val=0, max_val=top)

        def scatter(half):
            pool.indirect_dma_start(a.acc_dram, bass.IndirectOffsetOnAxis(m.sx[:, half:half + 1], 0), orow[half][:], None,
                                    bounds_check=last_row, oob_is_err=True, compute_op=ALU.add).then_inc(scattered[half], 16)

        def scatter_rows(n):
            with pool.If(n > 1):
                g.tensor_copy(m.sx[:], m.idx_s[:, bass.ds(value(column2, WIN - 2), 2)]).then_inc(sx_step, 1)
                pool.wait_ge(sx_step, n + 1)
            pool.wait_ge(psum_init, 4)
            pool.wait_ge(o_ready, n * 4 + 1)
            pool.sem_inc(pool_seen, 1)
            scatter(0)
            with pool.If(value(left2, S) > P):
                scatter(1)
                pool.wait_ge(scattered[1], value(scatters1, E * NWIN) * 16 + 16)
                pool.reg_add(scatters1, scatters1, 1)
            pool.wait_ge(scattered[0], n * 16 + 16)
            pool.sem_inc(rows_out, 1)
            pool.reg_mov(left2, left1)
            pool.reg_mov(column2, column1)

        def gather(half):
            pool.indirect_dma_start(xg[half][:], None, a.xn_dram, bass.IndirectOffsetOnAxis(m.gx[:, half:half + 1], 0),
                                    bounds_check=last_token, oob_is_err=False).then_inc(gathered[half], 16)

        def body(e, w, n, left):
            pool.wait_ge(x_full, n * 4 + 1)
            g.tensor_copy(m.gx[:], m.idx_g[:, bass.ds(e * 8 + w * 2, 2)]).then_inc(idx_step, 1)
            pool.wait_ge(idx_step, n + 1)
            pool.sem_inc(pool_seen, 1)
            gather(0)
            with pool.If(left > P):
                gather(1)
                pool.wait_ge(gathered[1], value(gathers1, E * NWIN) * 16 + 16)
                pool.reg_add(gathers1, gathers1, 1)
            pool.wait_ge(gathered[0], n * 16 + 16)
            pool.sem_inc(rows_in, 1)
            scatter_rows(n)
            pool.reg_mov(left1, left)
            pool.reg_mov(column1, e * 8 + w * 2)

        done = each_task(pool, m, "pool", body)
        n = pool.snap(done, min_val=0, max_val=E * NWIN)
        scatter_rows(n)
        scatter_rows(n + 1)

    @block.tensor
    def _(pe):
        pe.sem_inc(l1_full, JF)
        pe.sem_inc(l2_full, KC)
        pe.sem_inc(x_full, 1)
        pe.wait_ge(psum_init, 1)
        before = pe.alloc_register("before_pe")
        pe.reg_mov(before, 0)

        def transposed(n, k, per):
            pe.wait_ge((xt_act, xt_dve)[k // per % 2], n * 4 + per * (k // per // 2) + k % per + 1)

        def product(out, n, s, j, moving, ks, W, ready=None):
            if j % 2 == 0 and ks[0] == 0:
                pe.wait_ge(w_in[s], n * 16 + 16)
            for k in ks:
                if ready:
                    ready(k)
                last = nc.tensor.matmul(out, m.we[s][:, k, (j % 2) * P:(j % 2 + 1) * P], moving[:, k, 0:W], start=(k == 0), stop=(k == KC - 1))
            return last

        def transposes_in(n, width):
            pe.wait_ge(rows_in, n + 1)
            pe.wait_ge(o_ready, n * 4 + 1)
            count = parts(width)
            per = KC // count
            for q in range(count):
                if q >= 2:
                    pe.wait_ge((xt_act, xt_dve)[q % 2], n * 4 + 2)
                for i in range(per):
                    for half in range(width // P):
                        k = per * q + i
                        last = nc.tensor.transpose(m.ps[:, q % 2, width * i + P * half:width * i + P * half + P], (m.xg0, m.xg1)[half][:, k * P:(k + 1) * P], m.ident[:])
                last.then_inc(x_full, 4 // count)

        def transposes_out(n, width):
            pe.wait_ge(biased, n * KC + KC)
            count = parts(width)
            for o in range(count):
                half, q = divmod(o, 2)
                if o == 3:
                    pe.wait_ge(o_ready, n * 4 + 2)
                for i in range(4):
                    last = nc.tensor.transpose(m.ps[:, OUT_BANKS[o], P * i:P * i + P], m.outT[:, 4 * q + i, half * P:half * P + P], m.ident[:])
                last.then_inc(o_full, 4 // count)

        def task(n, W):
            transposes_in(n, P if W <= P else WIN)
            per = KC // parts(P if W <= P else WIN)
            for j in range(JF):
                bank = m.ps[:, 2 + j % 3, :]
                if j >= 3:
                    pe.wait_ge(lin_ok, n * JF + j - 2)
                for part in range(2):
                    last = product(bank[:, part * WIN:part * WIN + W], n, 2 * (j // 2) + part, j, m.xT, range(KC), W,
                                   ready=(lambda k: transposed(n, k, per)) if j == part == 0 else None)
                last.then_inc(l1_full, 1)
            by_width(pe, pe.snap(before, min_val=0, max_val=S), lambda width: transposes_out(n, width))
            early, late = range(JF - 2), range(JF - 2, JF)
            pe.wait_ge(acted, n * 4 + 5)
            for j in range(2):
                product(m.ps[:, 5 + j, 0:W], n, L1S, j, m.act, early, W)
            pe.wait_ge(acted, n * 4 + 6)
            for j in range(2):
                product(m.ps[:, 5 + j, 0:W], n, L1S, j, m.act, late, W).then_inc(l2_full, 1)
            for j in range(2, KC):
                if j == 2:
                    pe.wait_ge(o_ready, n * 4 + 5)
                if j >= 3:
                    pe.wait_ge(biased, n * KC + KC + j - 2)
                product(m.ps[:, 5 + j % 3, 0:W], n, L1S + j // 2, j, m.act, range(JF), W).then_inc(l2_full, 1)

        def body(e, w, n, left):
            def by_tokens(widths):
                if len(widths) == 1:
                    task(n, widths[0])
                    return
                lower, upper = widths[:len(widths) // 2], widths[len(widths) // 2:]
                with pe.If(left < lower[-1] + 1):
                    by_tokens(lower)
                with pe.If(left > lower[-1]):
                    by_tokens(upper)

            with pe.If(left < P + 1):
                task(n, P)
            with pe.If(left > P):
                by_tokens(WIDTHS[1:])
            pe.reg_mov(before, left)

        done = each_task(pe, m, "pe", body)
        n = pe.snap(done, min_val=0, max_val=E * NWIN)
        pe.wait_ge(o_ready, n * 4 + 1)
        pe.sem_inc(pe_seen, 1)
        by_width(pe, pe.snap(before, min_val=0, max_val=S), lambda width: transposes_out(n, width))

    @block.vector
    def _(dve):
        v = nc.vector
        v.memset(m.ps[:, 2:8, :], 0.0).then_inc(psum_init, 1)
        for buf in (m.outT, m.orow0, m.orow1):
            v.memset(buf[:], 0.0).then_inc(psum_init, 1)
        dve.wait_ge(psum_init, 4)
        dve.sem_inc(biased, KC)
        dve.sem_inc(acted, 2)

        def front(e, n, j, C):
            bank, b, i = m.ps[:, 2 + j % 3, :], (j // 2) % 2, j % 2
            if i == 0:
                dve.wait_ge(acted, n * 4 + j // 2 + 1)
            dve.wait_ge(l1_full, n * JF + JF + j + 1)
            v.tensor_scalar(m.glu[:, b, i, 0:C], bank[:, 0:C], m.b1T[:, bass.ds(e * 16 + j, 1)], LIMIT, ALU.add, ALU.min).then_inc(glu_ok, 1)
            v.tensor_scalar(m.lin[:, b, i, 0:C], bank[:, WIN:WIN + C], m.b1T[:, bass.ds(e * 16 + JF + j, 1)], LIMIT + 1, ALU.add, ALU.min).then_inc(lin_ok, 1)

        def back(n, p, C):
            b, js = p % 2, slice(2 * p, 2 * p + 2)
            sg, glu, lin = m.sg[:, b, :, 0:C], m.glu[:, b, :, 0:C], m.lin[:, b, :, 0:C]
            dve.wait_ge(swished, n * 4 + p + 1)
            v.tensor_tensor(sg, sg, glu, ALU.mult).then_inc(step_f, 1)
            dve.wait_ge(step_f, n * 4 + p + 1)
            dve.wait_ge(lin_ok, n * JF + 2 * p + 2)
            v.scalar_tensor_tensor(out=m.act[:, js, 0:C], in0=lin, scalar=1.0 - LIMIT, in1=sg, op0=ALU.max, op1=ALU.mult).then_inc(acted, 1)

        def body_of(e, n, C):
            count = parts(C)
            per = KC // count
            for q in range(1, count, 2):
                dve.wait_ge(x_full, n * 4 + 1 + (q + 1) * (4 // count))
                for i in range(per):
                    k = per * q + i
                    v.tensor_scalar(m.xT[:, k, 0:C], m.ps[:, 1, C * i:C * i + C], m.g_moe[:, k:k + 1], None, ALU.mult).then_inc(xt_dve, 1)
            for p in range(4):
                front(e, n, 2 * p, C)
                if p:
                    back(n, p - 1, C)
                front(e, n, 2 * p + 1, C)
            back(n, 3, C)
            for j in range(KC):
                dve.wait_ge(l2_full, n * KC + KC + j + 1)
                v.tensor_scalar(m.outT[:, j, 0:C], m.ps[:, 5 + j % 3, 0:C], m.b2T[:, bass.ds(e * KC + j, 1)], None, ALU.add).then_inc(biased, 1)

        def body(e, w, n, left):
            by_width(dve, left, lambda C: body_of(e, n, C))

        lin_bias = m.b1T[:].rearrange("p (e h j) -> p e h j", h=2, j=JF)[:, :, 1, :]
        v.tensor_scalar(lin_bias, lin_bias, 1.0, None, ALU.add).then_inc(psum_init, 1)
        dve.wait_ge(psum_init, 5)
        each_task(dve, m, "dve", body)

    @block.scalar
    def _(act):
        act.sem_inc(o_ready, 1)
        before, column = act.alloc_register("before_act"), act.alloc_register("column_act")
        act.reg_mov(before, 0)
        act.reg_mov(column, 0)

        def table(n, i):
            nc.scalar.activation(m.warm[:], m.half[:], ACT.Sigmoid).then_inc(warmed, 1)
            act.wait_ge(warmed, n * 2 + i + 1)

        def rows_of(n, width, warm=True):
            if warm:
                table(n, 1)
            count = parts(width)
            act.wait_ge(rows_out, n + 1)
            for o in range(count):
                half, q = divmod(o, 2)
                act.wait_ge(o_full, n * 4 + (o + 1) * (4 // count))
                act.sem_inc(act_seen, 1)
                nc.scalar.activation((m.orow0, m.orow1)[half][:, q * 512:(q + 1) * 512], m.ps[:, OUT_BANKS[o], :], ACT.Identity,
                                     scale=m.gate_l[:, bass.ds(act.snap(column, min_val=0, max_val=WIN - 2) + half, 1)]).then_inc(o_ready, 4 // count)

        def body_of(e, n, C):
            table(n, 0)
            count = parts(C)
            per = KC // count
            for q in range(0, count, 2):
                act.wait_ge(x_full, n * 4 + 1 + (q + 1) * (4 // count))
                for i in range(per):
                    k = per * q + i
                    nc.scalar.activation(m.xT[:, k, 0:C], m.ps[:, 0, C * i:C * i + C], ACT.Identity, scale=m.g_moe[:, k:k + 1]).then_inc(xt_act, 1)
            for p in range(4):
                act.wait_ge(glu_ok, n * JF + 2 * p + 2)
                act.wait_ge(acted, n * 4 + p + 1)
                nc.scalar.activation(m.sg[:, p % 2, :, 0:C], m.glu[:, p % 2, :, 0:C], ACT.Sigmoid, scale=ALPHA).then_inc(swished, 1)
            by_width(act, act.snap(before, min_val=0, max_val=S), lambda width: rows_of(n, width))

        def body(e, w, n, left):
            by_width(act, left, lambda C: body_of(e, n, C))
            act.reg_mov(before, left)
            act.reg_mov(column, e * 8 + w * 2)

        done = each_task(act, m, "act", body)
        n = act.snap(done, min_val=0, max_val=E * NWIN)
        by_width(act, act.snap(before, min_val=0, max_val=S), lambda width: rows_of(n, width, warm=False))


def phase_g(nc, block, m, a, sem):
    f_in, f_out, g_in = [sem(f"f_in{b}") for b in range(NB)], sem("f_out"), sem("g_in")
    sq_f, root_f, fin_ok, step_g, act_g = (sem(n) for n in ("sq_f", "root_f", "fin_ok", "step_g", "act_g"))

    @block.sync
    def _(sp):
        for b in range(NB):
            sp.dma_start(m.fin[:, b], a.acc_dram[b * P:(b + 1) * P]).then_inc(f_in[b], 16)
        for b in range(NB):
            sp.wait_ge(fin_ok, b + 1)
            sp.dma_start(a.out[0, b * P:(b + 1) * P], m.fout[:, b]).then_inc(f_out, 16)
        sp.wait_ge(f_out, 16 * NB)

    @block.scalar
    def _(act):
        ch = Chain(act, act_g)
        act.dma_start(m.gfin[:], a.norm_final.rearrange("(a n) -> a n", a=1).to_broadcast([P, D])).then_inc(g_in, 16)
        for b in range(NB):
            act.wait_ge(f_in[b], 16)
            ch.link(nc.scalar.activation(m.jf[:], m.fin[:, b], ACT.Square, accum_out=m.ss[:, b:b + 1]))
            act.sem_inc(sq_f, 1)

    @block.gpsimd
    def _(pool):
        ch = Chain(pool, step_g)
        for b in range(NB):
            pool.wait_ge(sq_f, b + 1)
            root(nc, m, ch, b, D).then_inc(root_f, 1)

    @block.vector
    def _(dve):
        dve.wait_ge(g_in, 16)
        for b in range(NB):
            dve.wait_ge(root_f, b + 1)
            nc.vector.scalar_tensor_tensor(out=m.fout[:, b], in0=m.fin[:, b], scalar=m.rs[:, b:b + 1], in1=m.gfin[:],
                                           op0=ALU.mult, op1=ALU.mult).then_inc(fin_ok, 1)


_SCRATCH = {"u_dram": (D_B, S), "kp_dram": (CH, G, 240), "line_dram": (H_A, LINE), "skew_dram": (H_A, P, LINE + 1), "y_dram": (G, CH, T, J),
            "xn_dram": (S, D), "acc_dram": (S + WIN, D)}


def hybrid_trunk_kernel(nc, aps):
    aps = dict(aps, **{name: nc.dram_tensor(name, shape, F32).ap() for name, shape in _SCRATCH.items()})
    a = namedtuple("Arrays", aps)(**aps)
    with ExitStack() as ctx:
        ctx.enter_context(nc.allow_non_contiguous_dma(reason="gains and parameters stand by column, a few KB in all"))
        m = memory(nc, ctx)

        for phase in PHASES:
            held = []

            def sem(name):
                held.append(nc.alloc_semaphore(name=name))
                return held[-1]

            with nc.Block() as block:
                phase(nc, block, m, a, sem)
            if phase is PHASES[-1]:
                held.extend(m.w_in)
            nc.clear_and_free_semaphores(held)
            nc.all_engine_barrier()


PHASES = [phase_a, phase_b, phase_c, phase_d, phase_e, phase_f, phase_g]

_STACKED = ("norm_mix", "w_in", "s5_a_re", "s5_a_im", "s5_b_re", "s5_b_im", "s5_c_re", "s5_c_im", "s5_log_dt", "s5_d",
            "w_glu", "b_glu", "g_out_attn", "g_out_ssm", "w_out", "norm_xattn", "norm_mem", "w_xq", "w_xkv", "w_xo",
            "norm_moe", "w_router", "b_router", "w1", "b1", "w2", "b2", "x", "mem")
_INS = _STACKED + ("rel_bias", "norm_final")


def kernel(**inputs):
    import numpy as _np
    import concourse.bacc as _bacc
    from concourse import mybir as _mybir
    from concourse.bass_utils import run_bass_kernel_spmd as _run

    nc = _bacc.Bacc("TRN2", target_bir_lowering=False, num_devices=1)
    arrays, aps = {}, {}
    for name in _INS:
        arr = _np.ascontiguousarray(inputs[name])
        arrays[f"in_{name}"] = arr
        ap = nc.dram_tensor(f"in_{name}", arr.shape, _mybir.dt.from_np(arr.dtype), kind="ExternalInput").ap()
        aps[name] = ap[0] if name in _STACKED else ap
    arrays["in_onehot"] = shape_constants()
    aps["onehot"] = nc.dram_tensor("in_onehot", (ONEHOT_ROWS, LINE), F32, kind="ExternalInput").ap()
    aps["out"] = nc.dram_tensor("out_0", (1, S, D), F32, kind="ExternalOutput").ap()
    hybrid_trunk_kernel(nc, aps)
    r = _run(nc, [arrays], core_ids=[0])
    return r.results[0]["out_0"]
```
